# Optimizing a Trainium2 kernel written in Bass

```python
import math
import jax
import jax.numpy as jnp
from jax import lax
import numpy as np

D_MODEL = 1024
BATCH = 1
SEQ = 512
DEPTH = 2

GRID_W = 64
CTX_LEN = 256
HEAD_DIM = 64
D_MIX = D_MODEL
A_HEADS = D_MIX // (2 * HEAD_DIM)
A_DIM = A_HEADS * HEAD_DIM
B_Q_HEADS = D_MIX // (2 * HEAD_DIM)
B_KV_HEADS = max(1, B_Q_HEADS // 4)
B_Q_DIM = B_Q_HEADS * HEAD_DIM
B_KV_DIM = B_KV_HEADS * HEAD_DIM
C_HEADS = D_MIX // HEAD_DIM
C_DIM = C_HEADS * HEAD_DIM
EVEN_SPLITS = (3 * A_DIM, A_DIM, A_HEADS, A_HEADS, A_HEADS, A_HEADS, B_Q_DIM, B_KV_DIM, B_KV_DIM)
IN_EVEN = sum(EVEN_SPLITS)
IN_ODD = 3 * C_DIM
SHORT_CONV = 3
DELTA_CHUNK = 64
Q_BLOCK = 128
NA_ROWS_MAX = 8
NA_COLS = 16
ROPE_THETA = 10000.0
N_EXPERTS = 16
EXPERT_FF = D_MODEL
EC_CAPACITY = 2
N_EVEN = (DEPTH + 1) // 2
N_ODD = DEPTH // 2
EPS = 1e-6
F32 = jnp.float32

kernel_name = 'hybrid_deltanet_gqa_natten_ecmoe_dit'

def rms_norm(x, g):
    xf = x.astype(F32)
    y = xf * lax.rsqrt(jnp.mean(xf * xf, axis=-1, keepdims=True) + EPS)
    return (y * g.astype(F32)).astype(x.dtype)

def l2_norm(x):
    return x * lax.rsqrt(jnp.sum(x * x, axis=-1, keepdims=True) + EPS)

def split_cols(p, sizes):
    return jnp.split(p, np.cumsum(sizes)[:-1].tolist(), axis=-1)

def modulate(x, g, shift, scale):
    return rms_norm(x, g) * (1 + scale) + shift

def axial_rope(n, dh):
    t = jnp.arange(n)
    rows = (t // GRID_W).astype(F32)
    cols = (t % GRID_W).astype(F32)
    n_freq = dh // 4
    inv = ROPE_THETA ** (-jnp.arange(n_freq, dtype=F32) / n_freq)
    ang = jnp.concatenate([rows[:, None] * inv, cols[:, None] * inv], axis=-1)
    return jnp.cos(ang), jnp.sin(ang)

def apply_rope(x, cos, sin):
    xf = x.astype(F32)
    x1, x2 = jnp.split(xf, 2, axis=-1)
    c, s = cos[:, None, :], sin[:, None, :]
    return jnp.concatenate([x1 * c - x2 * s, x1 * s + x2 * c], axis=-1).astype(x.dtype)

def short_conv(x, w):
    pad = w.shape[0] // 2
    return lax.conv_general_dilated(x, w[:, None, :].astype(x.dtype), (1,), [(pad, pad)],
                                    dimension_numbers=('NWC', 'WIO', 'NWC'),
                                    feature_group_count=x.shape[-1])

def deltanet_prep(qkv, a_f, b_f, a_b, b_b, conv_w, a_log, dt_bias):
    bn, n, _ = qkv.shape
    qkv = jax.nn.silu(short_conv(qkv, conv_w)).astype(F32)
    q, k, v = jnp.split(qkv, 3, axis=-1)
    q = l2_norm(q.reshape(bn, n, A_HEADS, HEAD_DIM)) * HEAD_DIM ** -0.5
    k = l2_norm(k.reshape(bn, n, A_HEADS, HEAD_DIM))
    v = v.reshape(bn, n, A_HEADS, HEAD_DIM)
    dirs = []
    for d, (a_in, b_in) in enumerate(((a_f, b_f), (a_b, b_b))):
        log_a = -jnp.exp(a_log[d].astype(F32)) * jax.nn.softplus(a_in.astype(F32) + dt_bias[d].astype(F32))
        beta = jax.nn.sigmoid(b_in.astype(F32))
        dirs.append((log_a, beta))
    return q, k, v, dirs

def delta_rule_chunked(q, k, v, log_a, beta, s0):
    bn, n, h, dk = q.shape
    dv = v.shape[-1]
    L = DELTA_CHUNK
    nc = n // L
    chunk = lambda t: t.reshape(bn, nc, L, h, t.shape[-1]).transpose(1, 0, 3, 2, 4)
    qc, kc, vc = chunk(q), chunk(k), chunk(v)
    g = jnp.cumsum(log_a.reshape(bn, nc, L, h).transpose(1, 0, 3, 2), axis=-1)
    bc = beta.reshape(bn, nc, L, h).transpose(1, 0, 3, 2)
    tri = np.tril(np.ones((L, L), dtype=bool))
    strict = np.tril(np.ones((L, L), dtype=bool), -1)
    gam = jnp.exp(jnp.where(tri, g[..., :, None] - g[..., None, :], -jnp.inf))
    kb = kc * bc[..., None]
    m = jnp.where(strict, jnp.einsum('nbhid,nbhjd->nbhij', kb, kc) * gam, 0.0)
    t_mat = m + jnp.eye(L, dtype=m.dtype)
    rhs = jnp.concatenate([vc * bc[..., None], kb * jnp.exp(g)[..., None]], axis=-1)
    sol = lax.linalg.triangular_solve(t_mat, rhs, left_side=True, lower=True, unit_diagonal=True)
    u, w = sol[..., :dv], sol[..., dv:]
    a_qk = jnp.einsum('nbhid,nbhjd->nbhij', qc, kc) * gam

    def step(s, inp):
        q_i, k_i, u_i, w_i, g_i, a_i = inp
        v_new = u_i - jnp.einsum('bhld,bhdv->bhlv', w_i, s)
        o_i = (jnp.einsum('bhld,bhdv->bhlv', q_i * jnp.exp(g_i)[..., None], s)
               + jnp.einsum('bhij,bhjv->bhiv', a_i, v_new))
        g_last = g_i[..., -1:]
        s = (s * jnp.exp(g_last)[..., None]
             + jnp.einsum('bhld,bhlv->bhdv', k_i * jnp.exp(g_last - g_i)[..., None], v_new))
        return s, o_i

    s_fin, o = lax.scan(step, s0, (qc, kc, u, w, g, a_qk))
    return s_fin, o.transpose(1, 0, 3, 2, 4).reshape(bn, n, h, dv)

def bidir_deltanet(lat, ctx_s):
    q_l, k_l, v_l, d_l = lat
    q_c, k_c, v_c, d_c = ctx_s
    s0 = jnp.zeros((q_l.shape[0], A_HEADS, HEAD_DIM, HEAD_DIM), F32)
    o_lat = jnp.zeros_like(v_l)
    o_ctx = jnp.zeros_like(v_c)
    for d in range(2):
        f = (lambda t: jnp.flip(t, axis=1)) if d == 1 else (lambda t: t)
        s_ctx, oc = delta_rule_chunked(f(q_c), f(k_c), f(v_c), f(d_c[d][0]), f(d_c[d][1]), s0)
        _, ol = delta_rule_chunked(f(q_l), f(k_l), f(v_l), f(d_l[d][0]), f(d_l[d][1]), s_ctx)
        o_lat = o_lat + f(ol)
        o_ctx = o_ctx + f(oc)
    return o_lat, o_ctx

def gated_out(o, z, g):
    bn, n, _ = z.shape
    y = rms_norm(o.astype(z.dtype), g) * jax.nn.silu(z.reshape(bn, n, A_HEADS, HEAD_DIM))
    return y.reshape(bn, n, A_DIM)

def attend_gqa(q, keys, vals):
    s = jnp.einsum('bqhgd,bkhd->bhgqk', q, keys).astype(F32)
    p = jax.nn.softmax(s, axis=-1).astype(vals.dtype)
    return jnp.einsum('bhgqk,bkhd->bqhgd', p, vals)

def gqa_latent(q, k, v, k_ctx, v_ctx):
    bn, n, hq, dh = q.shape
    hkv = k.shape[2]
    keys = jnp.concatenate([k_ctx, k], axis=1)
    vals = jnp.concatenate([v_ctx, v], axis=1)
    qb = q.reshape(bn, n // Q_BLOCK, Q_BLOCK, hkv, hq // hkv, dh).transpose(1, 0, 2, 3, 4, 5)
    o = lax.map(lambda q_blk: attend_gqa(q_blk, keys, vals), qb)
    return o.transpose(1, 0, 2, 3, 4, 5).reshape(bn, n, hq * dh)

def gqa_context(q, k, v):
    bn, n, hq, dh = q.shape
    hkv = k.shape[2]
    o = attend_gqa(q.reshape(bn, n, hkv, hq // hkv, dh), k, v)
    return o.reshape(bn, n, hq * dh)

def neighbourhood_latent(q, k, v, k_ctx, v_ctx, rpb):
    bn, n, h, dh = q.shape
    n_ctx = k_ctx.shape[1]
    rows = n // GRID_W
    wr = min(NA_ROWS_MAX, rows)
    r = np.arange(rows)
    row_start = np.clip(r - wr // 2, 0, rows - wr)
    row_off = row_start[:, None] + np.arange(wr)[None, :] - r[:, None]
    col = np.arange(GRID_W)
    col_idx = np.clip(col - NA_COLS // 2, 0, GRID_W - NA_COLS)[:, None] + np.arange(NA_COLS)[None, :]
    col_off = col_idx - col[:, None]
    k_grid = k.reshape(bn, rows, GRID_W, h, dh)
    v_grid = v.reshape(bn, rows, GRID_W, h, dh)
    q_rows = q.reshape(bn, rows, GRID_W, h, dh).transpose(1, 0, 2, 3, 4)

    def row_block(inp):
        q_r, r_start, r_off = inp
        k_band = lax.dynamic_slice_in_dim(k_grid, r_start, wr, axis=1)[:, :, col_idx]
        v_band = lax.dynamic_slice_in_dim(v_grid, r_start, wr, axis=1)[:, :, col_idx]
        bias = rpb[:, r_off[None, :, None] + (NA_ROWS_MAX - 1), col_off[:, None, :] + (NA_COLS - 1)]
        s_loc = jnp.einsum('bqhd,brqchd->bhqrc', q_r, k_band).astype(F32) + bias.astype(F32)[None]
        s_ctx = jnp.einsum('bqhd,bkhd->bhqk', q_r, k_ctx).astype(F32)
        s = jnp.concatenate([s_ctx, s_loc.reshape(bn, h, GRID_W, wr * NA_COLS)], axis=-1)
        p = jax.nn.softmax(s, axis=-1).astype(v.dtype)
        p_ctx = p[..., :n_ctx]
        p_loc = p[..., n_ctx:].reshape(bn, h, GRID_W, wr, NA_COLS)
        return (jnp.einsum('bhqk,bkhd->bqhd', p_ctx, v_ctx)
                + jnp.einsum('bhqrc,brqchd->bqhd', p_loc, v_band))

    o = lax.map(row_block, (q_rows, jnp.asarray(row_start, jnp.int32), jnp.asarray(row_off, jnp.int32)))
    return o.transpose(1, 0, 2, 3, 4).reshape(bn, n, h * dh)

def even_mixer(a_lat, a_ctx, w_in, conv_w, a_log, dt_bias, out_norm_g, q_norm_g, k_norm_g, w_out,
               cos, sin, need_ctx):
    pl = split_cols(a_lat @ w_in, EVEN_SPLITS)
    pc = split_cols(a_ctx @ w_in, EVEN_SPLITS)
    lat_a = deltanet_prep(pl[0], *pl[2:6], conv_w, a_log, dt_bias)
    ctx_a = deltanet_prep(pc[0], *pc[2:6], conv_w, a_log, dt_bias)
    o_lat_a, o_ctx_a = bidir_deltanet(lat_a, ctx_a)

    def qkv_b(p):
        bn, n, _ = p[6].shape
        q = rms_norm(p[6].reshape(bn, n, B_Q_HEADS, HEAD_DIM), q_norm_g) * HEAD_DIM ** -0.5
        k = rms_norm(p[7].reshape(bn, n, B_KV_HEADS, HEAD_DIM), k_norm_g)
        v = p[8].reshape(bn, n, B_KV_HEADS, HEAD_DIM)
        return q, k, v

    q_l, k_l, v_l = qkv_b(pl)
    q_c, k_c, v_c = qkv_b(pc)
    o_lat_b = gqa_latent(apply_rope(q_l, cos, sin), apply_rope(k_l, cos, sin), v_l, k_c, v_c)
    y_lat = jnp.concatenate([gated_out(o_lat_a, pl[1], out_norm_g), o_lat_b], axis=-1) @ w_out
    if not need_ctx:
        return y_lat, None
    o_ctx_b = gqa_context(q_c, k_c, v_c)
    y_ctx = jnp.concatenate([gated_out(o_ctx_a, pc[1], out_norm_g), o_ctx_b], axis=-1) @ w_out
    return y_lat, y_ctx

def odd_mixer(a_lat, a_ctx, w_in, rpb, w_out, need_ctx):
    def qkv_c(a):
        bn, n, _ = a.shape
        p = (a @ w_in).reshape(bn, n, 3, C_HEADS, HEAD_DIM)
        return p[:, :, 0] * HEAD_DIM ** -0.5, p[:, :, 1], p[:, :, 2]

    q_l, k_l, v_l = qkv_c(a_lat)
    q_c, k_c, v_c = qkv_c(a_ctx)
    y_lat = neighbourhood_latent(q_l, k_l, v_l, k_c, v_c, rpb) @ w_out
    if not need_ctx:
        return y_lat, None
    y_ctx = gqa_context(q_c, k_c, v_c) @ w_out
    return y_lat, y_ctx

def expert_choice_ffn(h, w_router, w_gate, w_up, w_down):
    bn, t, d = h.shape
    cap = max(1, EC_CAPACITY * t // N_EXPERTS)
    aff = jax.nn.softmax((h @ w_router).astype(F32), axis=-1)
    gate, idx = lax.top_k(jnp.swapaxes(aff, 1, 2), cap)
    xs = jax.vmap(lambda hb, ib: hb[ib])(h, idx)
    hid = jax.nn.silu(jnp.einsum('becd,edf->becf', xs, w_gate)) * jnp.einsum('becd,edf->becf', xs, w_up)
    y = jnp.einsum('becf,efd->becd', hid, w_down) * gate[..., None].astype(h.dtype)
    return jax.vmap(lambda yb, ib: jnp.zeros((t, d), yb.dtype).at[ib.reshape(-1)].add(yb.reshape(-1, d)))(y, idx)

def setup_inputs(seed: int = 0) -> dict:
    key = jax.random.key(seed)
    ks = jax.random.split(key, 26)

    def nrm(k, shape, scale):
        return jax.random.normal(k, shape, F32) * scale

    def gain(k, shape):
        return 1.0 + 0.02 * jax.random.normal(k, shape, F32)

    dt = jnp.exp(jax.random.uniform(ks[9], (N_EVEN, 2, A_HEADS), F32, math.log(1e-3), math.log(1e-1)))
    return {
        'x': nrm(ks[0], (BATCH, SEQ, D_MODEL), 1.0),
        'c': nrm(ks[1], (BATCH, D_MODEL), 1.0),
        'ctx': nrm(ks[2], (BATCH, CTX_LEN, D_MODEL), 1.0),
        'c_ctx': nrm(ks[3], (D_MODEL,), 1.0),
        'ada_w': nrm(ks[4], (DEPTH, D_MODEL, 6 * D_MODEL), 0.5 * D_MODEL ** -0.5),
        'ada_b': nrm(ks[5], (DEPTH, 6 * D_MODEL), 0.02),
        'ln1_g': gain(ks[6], (DEPTH, D_MODEL)),
        'ln2_g': gain(ks[7], (DEPTH, D_MODEL)),
        'even_w_in': nrm(ks[8], (N_EVEN, D_MODEL, IN_EVEN), D_MODEL ** -0.5),
        'even_conv_w': nrm(ks[10], (N_EVEN, SHORT_CONV, 3 * A_DIM), SHORT_CONV ** -0.5),
        'even_a_log': jnp.log(jax.random.uniform(ks[11], (N_EVEN, 2, A_HEADS), F32, 1.0, 16.0)),
        'even_dt_bias': dt + jnp.log(-jnp.expm1(-dt)),
        'even_out_norm_g': gain(ks[12], (N_EVEN, HEAD_DIM)),
        'even_q_norm_g': gain(ks[13], (N_EVEN, HEAD_DIM)),
        'even_k_norm_g': gain(ks[14], (N_EVEN, HEAD_DIM)),
        'even_w_out': nrm(ks[15], (N_EVEN, D_MIX, D_MODEL), D_MIX ** -0.5),
        'odd_w_in': nrm(ks[16], (N_ODD, D_MODEL, IN_ODD), D_MODEL ** -0.5),
        'odd_rpb': nrm(ks[17], (N_ODD, C_HEADS, 2 * NA_ROWS_MAX - 1, 2 * NA_COLS - 1), 0.2),
        'odd_w_out': nrm(ks[18], (N_ODD, C_DIM, D_MODEL), C_DIM ** -0.5),
        'router_w': nrm(ks[19], (DEPTH, D_MODEL, N_EXPERTS), D_MODEL ** -0.5),
        'expert_w_gate': nrm(ks[20], (DEPTH, N_EXPERTS, D_MODEL, EXPERT_FF), D_MODEL ** -0.5),
        'expert_w_up': nrm(ks[21], (DEPTH, N_EXPERTS, D_MODEL, EXPERT_FF), D_MODEL ** -0.5),
        'expert_w_down': nrm(ks[22], (DEPTH, N_EXPERTS, EXPERT_FF, D_MODEL), EXPERT_FF ** -0.5),
        'final_norm_g': gain(ks[23], (D_MODEL,)),
    }

def reference(x, c, ctx, c_ctx, ada_w, ada_b, ln1_g, ln2_g, even_w_in, even_conv_w, even_a_log,
              even_dt_bias, even_out_norm_g, even_q_norm_g, even_k_norm_g, even_w_out, odd_w_in,
              odd_rpb, odd_w_out, router_w, expert_w_gate, expert_w_up, expert_w_down, final_norm_g):
    cos, sin = axial_rope(x.shape[1], HEAD_DIM)
    h, hc = x, ctx
    s_lat = jax.nn.silu(c)
    s_ctx = jax.nn.silu(c_ctx)[None]
    for layer in range(DEPTH):
        need_ctx = layer < DEPTH - 1
        i = layer // 2
        mod_l = jnp.split((s_lat @ ada_w[layer] + ada_b[layer])[:, None, :], 6, axis=-1)
        mod_c = jnp.split((s_ctx @ ada_w[layer] + ada_b[layer])[:, None, :], 6, axis=-1)
        a_lat = modulate(h, ln1_g[layer], mod_l[0], mod_l[1])
        a_ctx = modulate(hc, ln1_g[layer], mod_c[0], mod_c[1])
        if layer % 2 == 0:
            y_lat, y_ctx = even_mixer(a_lat, a_ctx, even_w_in[i], even_conv_w[i], even_a_log[i],
                                      even_dt_bias[i], even_out_norm_g[i], even_q_norm_g[i],
                                      even_k_norm_g[i], even_w_out[i], cos, sin, need_ctx)
        else:
            y_lat, y_ctx = odd_mixer(a_lat, a_ctx, odd_w_in[i], odd_rpb[i], odd_w_out[i], need_ctx)
        moe = (router_w[layer], expert_w_gate[layer], expert_w_up[layer], expert_w_down[layer])
        h = h + mod_l[2] * y_lat
        h = h + mod_l[5] * expert_choice_ffn(modulate(h, ln2_g[layer], mod_l[3], mod_l[4]), *moe)
        if need_ctx:
            hc = hc + mod_c[2] * y_ctx
            hc = hc + mod_c[5] * expert_choice_ffn(modulate(hc, ln2_g[layer], mod_c[3], mod_c[4]), *moe)
    return rms_norm(h, final_norm_g)


_drawn_inputs = setup_inputs


def setup_inputs(seed=0):
    import zlib

    import numpy as np

    out = dict(_drawn_inputs(seed))
    spreads = {}
    factors = {'ada_b': 2.938,
     'ln1_g': 8.0,
     'ln2_g': 5.865,
     'even_out_norm_g': 8.0,
     'even_q_norm_g': 8.0,
     'even_k_norm_g': 8.0,
     'odd_rpb': 8.0,
     'final_norm_g': 2.904}
    for name, (base, spread) in spreads.items():
        noise = np.random.default_rng([zlib.crc32(name.encode()), seed]).standard_normal(out[name].shape)
        drawn = base * np.exp(spread * noise) if base else spread * noise
        out[name] = jnp.asarray(drawn.astype(out[name].dtype))
    for name, factor in factors.items():
        out[name] = (out[name] * factor).astype(out[name].dtype)
    return out
```

```python
from contextlib import ExitStack

import numpy as np
import concourse.bass as bass
from concourse import mybir
from concourse.alu_op_type import AluOpType as ALU

ACT = mybir.ActivationFunctionType
AX = mybir.AxisListType.X
F32 = mybir.dt.float32

P = 128
D = 1024
KT = D // P
CTX, LAT = 256, 512
TOK = CTX + LAT
CT, LT = CTX // P, LAT // P
NT = CT + LT
HD = 64
AH = 8
OH = 16
NE = 16
CAP_L, CAP_C = 2 * LAT // NE, 2 * CTX // NE
EPS = 1e-6
RING = 8
PADL = 64
AW = CTX + 2 * PADL + LAT
LO = CTX + PADL
AK = 2 * AH * HD
CONV_TILES = 3 * AH * HD // P
XW = 1 + CTX + 1 + LAT + 1
REST = 288
MASKS = 9
NEG = -1.0e30


def host_constants():
    j, i = np.meshgrid(np.arange(P), np.arange(P), indexing="ij")
    masks = np.zeros((P, 2, MASKS, P), np.float32)
    for d in range(2):
        row, col = (j, i) if d == 0 else (i, j)
        masks[:, d, 0] = col > row
        masks[:, d, 1] = col >= row
        masks[:, d, 2] = (j == i) * 1.0 - ((col == row + 1) & (col % 2 == 1))
        for n in range(1, 7):
            s = 2 ** n
            low = (row // (2 * s) == col // (2 * s)) & (row // s % 2 == 1) & (col // s % 2 == 0)
            masks[:, d, 2 + n] = (j == i) * 1.0 - low
    t = np.arange(LAT)
    inv = (10000.0 ** (-np.arange(16, dtype=np.float32) / np.float32(16))).astype(np.float32)
    ang = np.concatenate([(t // 64).astype(np.float32)[:, None] * inv,
                          (t % 64).astype(np.float32)[:, None] * inv], -1)
    rope = np.stack([np.cos(ang), np.sin(ang)], 1).astype(np.float32)
    rope = rope.reshape(LT, P, 2, 32).transpose(1, 0, 2, 3)
    base = np.concatenate([np.eye(P, dtype=np.float32), np.ones((P, P), np.float32),
                           np.tile(np.arange(1, 65, dtype=np.float32), (P, 1)),
                           np.arange(P, dtype=np.float32)[:, None]], 1)
    sel = np.zeros((P, 8, P), np.float32)
    for q in range(4):
        for v in range(2):
            sel[32 * q + v, 2 * q + v] = 1.0
    return {"base": base, "masks": masks.reshape(P, -1), "rope": np.ascontiguousarray(rope).reshape(P, -1),
            "sel": sel.reshape(P, -1)}


def bias_windows(rpb):
    q, wi = np.meshgrid(np.arange(128), np.arange(256), indexing="ij")
    out = []
    for j in (0, 1, 3):
        qc, qr = 16 * j + q // 8, q % 8
        kc, kr = 16 * j - 8 + wi // 8, wi % 8
        first = np.clip(qc - 8, 0, 48)
        near = (kc >= first) & (kc < first + 16)
        co = np.clip(kc - qc + 15, 0, 30)
        out.append(np.where(near[None], rpb[:, kr - qr + 7, co], np.float32(-1.0e30)).transpose(1, 0, 2))
    return np.ascontiguousarray(np.stack(out), dtype=np.float32)


def lay_out(a):
    c = np.ascontiguousarray
    w = a["even_w_in"][0]
    perm = np.concatenate([np.arange(64) + 64 * h for h in (0, 4, 1, 5, 2, 6, 3, 7)])
    tiles = lambda m, n: c(m.reshape(m.shape[0] // (n * P), n, P, m.shape[1]).transpose(0, 2, 1, 3).reshape(-1, P, n * m.shape[1]))
    chan = lambda m: c(m.reshape(KT, P, KT, P).transpose(2, 1, 0, 3).reshape(KT, P, KT * P))
    adab = np.zeros((2, P, 3, 512), np.float32)
    for l in range(2):
        for i in range(6):
            for h in range(2):
                q = 2 * (i // 3) + h
                adab[l, 32 * q:32 * q + 2, i % 3] = a["ada_b"][l, i * 1024 + h * 512:i * 1024 + (h + 1) * 512]
    d = dict(
        x=c(a["x"][0]), ctx=c(a["ctx"][0]),
        cT=c(np.stack([a["c"][0], a["c_ctx"]]).reshape(2, KT, P).transpose(2, 1, 0).reshape(P, -1)),
        ada_w=a["ada_w"], adab=adab.reshape(2, P, 1536),
        lnT=c(np.stack([a["ln1_g"][0], a["ln2_g"][0], a["ln1_g"][1], a["ln2_g"][1]]).reshape(4, KT, P).transpose(2, 0, 1).reshape(P, -1)),
        wrest=tiles(c(np.concatenate([w[:, 2592:2848], w[:, 2048:2080]], 1)), 2),
        wq=tiles(c(w[:, 2080:2592][:, perm]), 2), wz=tiles(c(w[:, 1536:2048]), 2),
        wconv=c(w[:, :1536].reshape(KT, P, CONV_TILES, P).transpose(2, 1, 0, 3).reshape(CONV_TILES, P, KT * P)),
        cw=c(a["even_conv_w"][0].reshape(3, CONV_TILES, P).transpose(2, 1, 0).reshape(P, -1)),
        dt_bias=c(a["even_dt_bias"][0].reshape(16)), a_log=c(a["even_a_log"][0].reshape(16)),
        go=c(a["even_out_norm_g"][0]), gq=c(a["even_q_norm_g"][0]), gk=c(a["even_k_norm_g"][0]),
        wout0=a["even_w_out"][0],
        router=c(a["router_w"].reshape(2, KT, P, 16).transpose(0, 2, 1, 3).reshape(2, P, -1)),
        expert_w_gate=a["expert_w_gate"], expert_w_up=a["expert_w_up"], expert_w_down=a["expert_w_down"],
        oq=chan(a["odd_w_in"][0][:, 0:1024]), ok=chan(a["odd_w_in"][0][:, 1024:2048]), wv=c(a["odd_w_in"][0][:, 2048:]),
        wout1=a["odd_w_out"][0], fin_g=a["final_norm_g"], bias=bias_windows(a["odd_rpb"][0]),
    )
    d.update(host_constants())
    return d


class Chain:

    def __init__(self, eng, sem):
        self.eng, self.sem, self.count = eng, sem, 0

    def __call__(self, ins):
        self.mark(ins)
        self.wait()

    def mark(self, ins):
        ins.then_inc(self.sem, 1)
        self.count += 1

    def wait(self):
        self.eng.wait_ge(self.sem, self.count)


def bc(ap, shape):
    return ap.broadcast_to(shape)


def build(nc, t, out):
    ctx = ExitStack()
    with ctx:
        def sb(name, words):
            return ctx.enter_context(nc.sbuf_tensor(name + "_sb", [P, words], F32))

        def sem(name):
            return ctx.enter_context(nc.semaphore(name))

        ps = ctx.enter_context(nc.psum_tensor("ps", [P, 8, 512], F32))
        hs = sb("h", NT * D)
        H = hs[:, :].rearrange("p (t d) -> p t d", t=NT)
        ring_t = sb("ring", RING * D)
        ring = ring_t[:, :].rearrange("p (u n) -> p u n", u=RING)
        base_t = sb("base", 321)
        IDENT, ONES, SLOT, PIDX = base_t[:, 0:P], base_t[:, P:2 * P], base_t[:, 256:320], base_t[:, 320:321]
        gate_t = sb("gates", 4 * D)
        GATE = gate_t[:, :].rearrange("p (w v n) -> p w v n", w=2, v=2)
        modT_t = sb("modT", 2 * 6 * KT)
        modT = modT_t[:, :].rearrange("p (v i k) -> p v i k", v=2, i=6)
        sT_t = sb("sT", KT * 32)
        sT = sT_t[:, :].rearrange("p (k m) -> p k m", k=KT)
        lnT_t = sb("lnT", 4 * KT)
        lnT = lnT_t[:, :].rearrange("p (w k) -> p w k", w=4)
        scale_t = sb("scaleT", 2 * 2 * KT)
        AT = scale_t[:, :].rearrange("p (w v k) -> p w v k", w=2, v=2)
        stat_t = sb("stats", 32)
        eps_t = sb("eps", 2)
        EPSC, ONE = eps_t[:, 0:1], eps_t[:, 1:2]
        WORK = 52900 - NT * D - RING * D - 321 - 4 * D - 96 - 256 - 32 - 32 - 32 - 2 - 1536
        rows_sb = sb("modrows", 3 * 512)
        work = sb("work", WORK)

        def region(first, words, pattern=None, **kw):
            assert first + words <= WORK, (first, words, WORK)
            ap = work[:, first:first + words]
            return ap.rearrange(pattern, **kw) if pattern else ap

        gb_rows = nc.dram_tensor("gb_rows", [32, TOK], F32, kind="Internal").ap()

        w_land = [sem(f"w_land{s}") for s in range(RING)]
        w_free = sem("w_free")

        stream = []

        def add(kind, *args):
            stream.append((kind, args))
            return len(stream) - 1

        def landed(pe, u):
            pe.wait_ge(w_land[u % RING], 16 * (u // RING + 1))
            return ring[:, u % RING, :]

        small_in = sem("small_in")
        consts_in = sem("consts_in")
        x_in = sem("x_in")
        s_silu = sem("s_silu")
        sT_zero = sem("sT_zero")
        rows_in = sem("rows_in")
        ada1_in = sem("ada1_in")
        rows_ok = sem("rows_ok")
        modT_mm = sem("modT_mm")
        modT_ok = sem("modT_ok")
        gate_mm = sem("gate_mm")
        gate_ok = sem("gate_ok")
        dve_step, pool_step = sem("dve_step"), sem("pool_step")
        rows_t = rows_sb
        ROWS = rows_t[:, :].rearrange("p (r n) -> p r n", r=3)
        SEL = region(25000, 8 * P, "p (s m) -> p s m", s=8)
        cT = region(24000, 2 * KT)
        cT_e = region(24020, 2 * KT)

        def LB(l):
            return l

        def ada_unit(l, n):
            r, k, i = n // 16, n % 16 // 2, n // 16 + 3 * (n % 2)
            return t["ada_w"][l, k * P:(k + 1) * P, i * D:(i + 1) * D], r, k, i

        def ada_matmuls(pe, l, u, n, bank):
            _, r, k, i = ada_unit(l, n)
            w = landed(pe, u)
            for a in range(2):
                q = 2 * (i // 3) + a
                mm = pe.matmul(ps[32 * q:32 * q + 32, bank, :], sT[:, k, :], w[:, a * 512:(a + 1) * 512],
                               start=(k == 0), stop=(k == KT - 1))
            mm.then_inc(w_free, 1)

        def ada_finish_pe(pe, l, dve_wait):
            pe.wait_ge(rows_ok, 3 * LB(l) + 3)
            for r in range(3):
                for m in range(4):
                    tr = pe.transpose(ps[:, 3 + r, m * P:(m + 1) * P], ROWS[:, r, m * P:(m + 1) * P], IDENT)
            tr.then_inc(modT_mm, 1)
            for g in range(4):
                w, v = g // 2, g % 2
                if g > 0:
                    pe.wait_ge(gate_ok, 4 * LB(l) + g)
                for a in range(2):
                    mm = pe.matmul(ps[:, 6 + a, :], SEL[:, 2 * (2 * w + a) + v, :], ROWS[:, 2, :],
                                   start=True, stop=True)
                mm.then_inc(gate_mm, 1)

        def ada_finish_act(act, l):
            for g in range(4):
                w, v = g // 2, g % 2
                act.wait_ge(gate_mm, 4 * LB(l) + g + 1)
                nc.scalar.copy(GATE[:, w, v, :].rearrange("p (a n) -> p a n", a=2), ps[:, 6:8, :]) \
                    .then_inc(gate_ok, 1)

        def ada_rows_dve(dve, l, r, bank):
            if r == 0:
                dve.wait_ge(ada1_in if l else rows_in, 16)
            dve.wait_ge(w_free, U_ADA[l] + 16 * (r + 1))
            nc.vector.tensor_tensor(ROWS[:, r, :], ps[:, bank, :], ROWS[:, r, :], ALU.add).then_inc(rows_ok, 1)

        def ada_finish_dve(dve, l, step):
            dve.wait_ge(modT_mm, 1 * LB(l) + 1)
            for r in range(3):
                for m in range(4):
                    for a in range(2):
                        src = ps[:, 3 + r, m * P:(m + 1) * P].rearrange("p (g b v) -> p g b v", g=2, b=2)
                        src = src[:, a, :, 0:2].rearrange("p b v -> p v b")
                        dst = modT[:, :, r + 3 * a, m::4]
                        last = nc.vector.tensor_copy(dst, src)
            last.then_inc(modT_ok, 1)
            dve.wait_ge(modT_ok, 2 * LB(l) + 1)
            dve.wait_ge(small_in, 16 * SMALL_IN)
            for w in range(2):
                for v in range(2):
                    last = nc.vector.scalar_tensor_tensor(AT[:, w, v, :], modT[:, v, 1 + 3 * w, :], 1.0,
                                                          lnT[:, 2 * l + w, :], ALU.add, ALU.mult)
            last.then_inc(modT_ok, 1)

        NORMS = ["n1_0", "n2_0", "n1_1", "n2_1"]
        sq_ok = sem("sq_ok")
        rt_ok = sem("rt_ok")
        rc_ok = sem("rc_ok")
        xn_ok = sem("xn_ok")
        tr_ok = sem("tr_ok")
        am_ok = sem("am_ok")
        ac_ok = sem("ac_ok")

        def before(n):
            done = NORMS[:NORMS.index(n)]
            return len(done), sum(LT if x == "n2_1" else NT for x in done), KT * sum(x != "n2_1" for x in done)

        def norm_act(act, n, tiles, junk, ctx_too, w, A, ready):
            runs, tiles0, ctx0 = before(n)
            for i, tt in enumerate(tiles):
                ready(act, i)
                if i >= 2:
                    act.wait_ge(sq_ok, tiles0 + i - 1)
                nc.scalar.activation(junk[:, i % 2, :], H[:, tt, :], ACT.Square, accum_out=stat_t[:, tt:tt + 1]) \
                    .then_inc(sq_ok, 1)
            act.wait_ge(sq_ok, tiles0 + len(tiles))
            act.wait_ge(dve_eps, 1)
            nc.scalar.activation(stat_t[:, 8 + tiles[0]:8 + NT], stat_t[:, tiles[0]:NT], ACT.Sqrt,
                                 bias=EPSC, scale=1.0 / D).then_inc(rt_ok, 1)
            if not ctx_too:
                return
            l = int(n[-1])
            act.wait_ge(modT_ok, 2 * LB(l) + 2)
            for k in range(KT):
                act.wait_ge(tr_ok, KT * runs + k + 1)
                nc.scalar.activation(A[:, k, 0:CTX], ps[:, 2 * (k % 2) + 1, 0:CTX], ACT.Identity,
                                     scale=AT[:, w, 1, k:k + 1], bias=modT[:, 1, 3 * w, k:k + 1]) \
                    .then_inc(ac_ok, 1)

        def norm_dve(dve, n, tiles, xn, w, A, by_column=False):
            runs, tiles0, ctx0 = before(n)
            dve.wait_ge(rt_ok, runs + 1)
            nc.vector.reciprocal(stat_t[:, 16 + tiles[0]:16 + NT], stat_t[:, 8 + tiles[0]:8 + NT]).then_inc(rc_ok, 1)
            dve.wait_ge(rc_ok, runs + 1)
            for tt in tiles:
                nc.vector.tensor_scalar(xn[:, tt, :], H[:, tt, :], stat_t[:, 16 + tt:17 + tt], None, ALU.mult) \
                    .then_inc(xn_ok, 1)
            l = int(n[-1])
            dve.wait_ge(modT_ok, 2 * LB(l) + 2)
            for k in range(KT):
                dve.wait_ge(tr_ok, KT * runs + k + 1)
                dst, src = A[:, k, LO:LO + LAT], ps[:, 2 * (k % 2), :]
                if by_column:
                    dst = dst.rearrange("p (c r) -> p r c", r=8)
                    src = src.rearrange("p (r c) -> p r c", r=8)
                nc.vector.tensor_scalar(dst, src, AT[:, w, 0, k:k + 1], modT[:, 0, 3 * w, k:k + 1],
                                        ALU.mult, ALU.add).then_inc(am_ok, 1)

        def norm_pe(pe, n, tiles, xn, ctx_too):
            runs, tiles0, ctx0 = before(n)
            pe.wait_ge(xn_ok, tiles0 + len(tiles))
            for k in range(KT):
                if k >= 2:
                    pe.wait_ge(am_ok, KT * runs + k - 1)
                    if ctx_too:
                        pe.wait_ge(ac_ok, ctx0 + k - 1)
                for tt in tiles:
                    bank, col = (2 * (k % 2) + 1, tt * P) if tt < CT else (2 * (k % 2), (tt - CT) * P)
                    tr = pe.transpose(ps[:, bank, col:col + P], xn[:, tt, k * P:(k + 1) * P], IDENT)
                tr.then_inc(tr_ok, 1)

        dve_eps = sem("dve_eps")
        SMALL_IN = 2

        A = region(0, KT * AW, "p (k t) -> p k t", k=KT)
        XN = region(7168, NT * D, "p (t d) -> p t d", t=NT)
        JUNK = region(13312, 2 * D, "p (b d) -> p b d", b=2)
        QKB = region(7168, NT * 640, "p (t n) -> p t n", t=NT)
        VB = region(11008, NT * P, "p (t n) -> p t n", t=NT)
        ZS = region(11776, NT * 512, "p (t n) -> p t n", t=NT)
        AB = region(14848, NT * 32, "p (t d w h) -> p t d w h", t=NT, d=2, w=2)
        GB = region(15040, NT * 32, "p (t d w h) -> p t d w h", t=NT, d=2, w=2)

        def small(n, words=96):
            return region(15232 + 96 * n, words)

        LA, TMPG, TMPE = small(0), small(1), small(2)
        EG, EK, EGL, GLAST = small(3), small(4), small(5), small(6)
        SS, RS = small(7, 192), region(16096, 104)
        RSUM = RS[:, 0:48]
        NEGM = RS[:, 48:50]
        RINV = RS[:, 56:104]
        QTP = region(16200, 8 * TOK, "p (s t) -> p s t", s=8)
        KTB = region(22344, TOK)
        PB = region(23112, 2 * TOK, "p (b n) -> p b n", b=2)
        PT = region(24648, 2 * TOK, "p (b n) -> p b n", b=2)
        ROPE = region(26184, 256, "p (t w c) -> p t w c", t=LT, w=2)
        RTMP = region(26440, 4 * 320, "p (w n) -> p w n", w=4)
        GAIN = region(27720, 640)
        SQJ = region(28360, 1280, "p (b n) -> p b n", b=2)
        ROWT = region(29640, TOK)
        DTB, ALOG = region(30408, 16), region(30424, 16)
        GO = region(30440, 64)
        CW = region(30504, CONV_TILES * 3, "p (c w) -> p c w", w=3)
        YC = H

        U_ADA = [0, 0]
        for n in range(48):
            add("ada", 0, n)
        U_BLK = []
        for b in range(3):
            U_BLK.append(len(stream))
            for k2 in range(4):
                add("blk", b, k2)
        U_ADA[1] = len(stream)
        for n in range(48):
            add("ada", 1, n)
        U_CONV = len(stream)
        for c in range(CONV_TILES):
            add("conv", c)
        U_OUT0 = len(stream)
        for k in range(KT):
            add("wout0", k)

        tp_mm, tp_dve, tp_act = sem("tp_mm"), sem("tp_dve"), sem("tp_act")
        ab_x, ab_e, ab_la, ab_beta = sem("ab_x"), sem("ab_e"), sem("ab_la"), sem("ab_beta")
        g_mm, g_act, g_diff, g_ek, g_tr, g_rowT, g_rows = (sem(n) for n in (
            "g_mm", "g_act", "g_diff", "g_ek", "g_tr", "g_rowT", "g_rows"))
        bsq_ok, bss_ok, brt_ok, bqk_ok, bqt_mm, bqt_dve, bqt_act = (sem(n) for n in (
            "bsq_ok", "bss_ok", "brt_ok", "bqk_ok", "bqt_mm", "bqt_dve", "bqt_act"))
        gq_s, gq_max, gq_exp, gq_tr, gq_pta, gq_ptd, gq_pv, gq_o, gq_rinv = (sem(n) for n in (
            "gq_s", "gq_max", "gq_exp", "gq_tr", "gq_pta", "gq_ptd", "gq_pv", "gq_o", "gq_rinv"))
        qtp_zero, qtp_load = sem("qtp_zero"), sem("l0_rows_in")
        WIDTH = [REST, 512, 512]

        def tok_cols(tt):
            return tt * P if tt < CT else LO + (tt - CT) * P

        def proj_pe(pe):
            pe.wait_ge(am_ok, KT)
            pe.wait_ge(ac_ok, KT)
            for b in range(3):
                N = WIDTH[b]
                for tt in range(NT):
                    j = b * NT + tt
                    if j >= 4:
                        if j - 4 < NT:
                            pe.wait_ge(tp_dve, j - 3)
                        else:
                            pe.wait_ge(tp_act, j - 3 - NT)
                    for k in range(KT):
                        w = landed(pe, U_BLK[b] + k // 2)
                        mm = pe.matmul(ps[:, j % 4, 0:N], A[:, k, tok_cols(tt):tok_cols(tt) + P],
                                       w[:, (k % 2) * N:(k % 2 + 1) * N], start=(k == 0), stop=(k == KT - 1))
                        if tt == NT - 1 and k % 2 == 1:
                            mm.then_inc(w_free, 1)
                    if tt < NT - 1:
                        mm.then_inc(tp_mm, 1)

        def projected(eng, b, tt):
            if tt < NT - 1:
                eng.wait_ge(tp_mm, b * (NT - 1) + tt + 1)
            else:
                eng.wait_ge(w_free, U_BLK[b] + 4)

        def proj_act(act):
            for j in range(NT, 3 * NT):
                tt = j % NT
                projected(act, j // NT, tt)
                if j < 2 * NT:
                    nc.scalar.copy(QKB[:, tt, 0:512], ps[:, j % 4, :]).then_inc(tp_act, 1)
                else:
                    nc.scalar.activation(ZS[:, tt, :], ps[:, j % 4, :], ACT.Silu).then_inc(tp_act, 1)

        def proj_dve(dve):
            for tt in range(NT):
                projected(dve, 0, tt)
                nc.vector.tensor_copy(QKB[:, tt, 512:640], ps[:, tt % 4, 0:P])
                nc.vector.tensor_copy(VB[:, tt, :], ps[:, tt % 4, P:2 * P])
                nc.vector.tensor_copy(AB[:, tt].rearrange("p d w h -> p (d w h)"), ps[:, tt % 4, 2 * P:REST]) \
                    .then_inc(tp_dve, 1)

        la3 = LA.rearrange("p (t d h) -> p t d h", t=NT, d=2)

        def v4(ap):
            return ap.rearrange("p (t d h) -> p t d h", t=NT, d=2)

        def gates_dve(dve, step):
            dve.wait_ge(tp_dve, NT)
            dve.wait_ge(qtp_load, 16 * 7)
            nc.vector.tensor_tensor(v4(LA), AB[:, :, :, 0, :],
                                    bc(DTB.rearrange("p (d h) -> p d h", d=2).unsqueeze(1), [P, NT, 2, 8]),
                                    ALU.add).then_inc(ab_x, 1)
            dve.wait_ge(ab_e, 5)
            step(nc.vector.scalar_tensor_tensor(LA, LA, 0.0, TMPE, ALU.max, ALU.add))
            nc.vector.scalar_tensor_tensor(LA.rearrange("p (t m) -> p t m", t=NT),
                                           LA.rearrange("p (t m) -> p t m", t=NT), -1.0,
                                           bc(ALOG.unsqueeze(1), [P, NT, 16]), ALU.mult, ALU.mult).then_inc(ab_la, 1)
            step(nc.vector.tensor_scalar(v4(TMPG), GB[:, :, :, 1, :], 1.0, None, ALU.add))
            nc.vector.reciprocal(GB[:, :, :, 1, :], v4(TMPG)).then_inc(ab_beta, 1)
            dve.wait_ge(g_mm, 1)
            step(nc.vector.tensor_copy(GB[:, :, :, 0, :], v4(ps[:, 7, 0:96])))
            nc.vector.tensor_tensor(v4(GLAST), v4(ps[:, 7, 96:192]), GB[:, :, :, 0, :], ALU.subtract).then_inc(g_diff, 1)
            dve.wait_ge(g_tr, 1)
            nc.vector.tensor_copy(ROWT[0:32, 0:512], ps[0:32, 5, :])
            nc.vector.tensor_copy(ROWT[0:32, 512:768], ps[0:32, 6, 0:256]).then_inc(g_rowT, 1)

        def gates_act(act):
            act.wait_ge(ab_x, 1)
            act.wait_ge(qtp_load, 16 * 7)
            nc.scalar.activation(TMPG, LA, ACT.Abs).then_inc(ab_e, 1)
            act.wait_ge(ab_e, 1)
            nc.scalar.activation(TMPE, TMPG, ACT.Exp, scale=-1.0).then_inc(ab_e, 1)
            nc.scalar.activation(ALOG, ALOG, ACT.Exp).then_inc(ab_e, 1)
            nc.scalar.activation(GB[:, :, :, 1, :], AB[:, :, :, 1, :], ACT.Exp, scale=-1.0).then_inc(ab_e, 1)
            act.wait_ge(ab_e, 4)
            nc.scalar.activation(TMPE, TMPE, ACT.Ln, bias=ONE).then_inc(ab_e, 1)
            act.wait_ge(g_diff, 1)
            nc.scalar.activation(EG, ps[:, 7, 0:96], ACT.Exp)
            nc.scalar.activation(EGL, ps[:, 7, 96:192], ACT.Exp).then_inc(g_act, 1)
            nc.scalar.activation(EK, GLAST, ACT.Exp).then_inc(g_ek, 1)

        def gates_pe(pe):
            pe.wait_ge(ab_la, 1)
            pe.wait_ge(masks0_in, 16)
            pe.wait_ge(gate_ok, 4)
            for tt in range(NT):
                for d in range(2):
                    c = tt * 16 + d * 8
                    pe.matmul(ps[:, 7, c:c + 8], MSUM[:, d, :], LA[:, c:c + 8], start=True, stop=True)
                mm = pe.matmul(ps[:, 7, 96 + tt * 16:112 + tt * 16], ONES, LA[:, tt * 16:tt * 16 + 16],
                               start=True, stop=True)
            mm.then_inc(g_mm, 1)
            pe.wait_ge(ab_beta, 1)
            pe.wait_ge(g_diff, 1)
            for tt in range(NT):
                tr = pe.transpose(ps[0:32, 5 + tt // 4, tt % 4 * P:(tt % 4 + 1) * P],
                                  GB[:, tt].rearrange("p d w h -> p (d w h)"), IDENT)
            tr.then_inc(g_tr, 1)

        masks0_in = sem("masks0_in")
        MSUM = region(30540, 256, "p (d n) -> p d n", d=2)

        def bnorm_act(act):
            act.wait_ge(tp_dve, NT)
            act.wait_ge(tp_act, NT)
            for tt in range(NT):
                if tt >= 2:
                    act.wait_ge(bss_ok, tt - 1)
                nc.scalar.activation(SQJ[:, tt % 2, :], QKB[:, tt, :], ACT.Square).then_inc(bsq_ok, 1)
            act.wait_ge(bss_ok, NT)
            nc.scalar.activation(SS[:, 64:124], SS[:, 0:60], ACT.Sqrt, bias=EPSC, scale=1.0 / HD).then_inc(brt_ok, 1)

        def bnorm_dve(dve, step):
            for tt in range(NT):
                dve.wait_ge(bsq_ok, tt + 1)
                nc.vector.tensor_reduce(SS[:, tt * 10:tt * 10 + 10], SQJ[:, tt % 2, :].rearrange(
                    "p (h d) -> p h d", d=HD), AX, ALU.add).then_inc(bss_ok, 1)
            step(nc.vector.tensor_scalar(GAIN[:, 0:512], GAIN[:, 0:512], HD ** -0.5, None, ALU.mult))
            dve.wait_ge(brt_ok, 1)
            step(nc.vector.reciprocal(SS[:, 128:188], SS[:, 64:124]))
            for tt in range(NT):
                x = QKB[:, tt, :].rearrange("p (h d) -> p h d", d=HD)
                step(nc.vector.tensor_tensor(x, x, bc(SS[:, 128 + tt * 10:138 + tt * 10].unsqueeze(2), [P, 10, HD]),
                                             ALU.mult))
                if tt < CT:
                    nc.vector.tensor_tensor(QKB[:, tt, :], QKB[:, tt, :], GAIN, ALU.mult).then_inc(bqk_ok, 1)
                    continue
                step(nc.vector.tensor_tensor(QKB[:, tt, :], QKB[:, tt, :], GAIN, ALU.mult))
                x1, x2 = x[:, :, 0:32], x[:, :, 32:64]
                cos, sin = (bc(ROPE[:, tt - CT, w, :].unsqueeze(1), [P, 10, 32]) for w in range(2))
                T = [RTMP[:, w, :].rearrange("p (h c) -> p h c", c=32) for w in range(4)]
                nc.vector.tensor_tensor(T[0], x1, cos, ALU.mult)
                nc.vector.tensor_tensor(T[1], x2, sin, ALU.mult)
                nc.vector.tensor_tensor(T[2], x1, sin, ALU.mult)
                step(nc.vector.tensor_tensor(T[3], x2, cos, ALU.mult))
                nc.vector.tensor_tensor(x1, T[0], T[1], ALU.subtract)
                nc.vector.tensor_tensor(x2, T[2], T[3], ALU.add).then_inc(bqk_ok, 1)

        def btrans_pe(pe):
            for tt in range(NT):
                pe.wait_ge(bqk_ok, tt + 1)
                if tt == 0:
                    pe.wait_ge(tp_act, 2 * NT)
                b = 2 * (tt % 2)
                if tt >= 2:
                    pe.wait_ge(bqt_dve, tt - 1)
                    pe.wait_ge(bqt_act, tt - 1)
                for c in range(5):
                    tr = pe.transpose(ps[:, b + c // 4, c % 4 * P:(c % 4 + 1) * P], QKB[:, tt, c * P:(c + 1) * P], IDENT)
                tr.then_inc(bqt_mm, 1)

        def btrans_dve(dve):
            dve.wait_ge(qtp_zero, 1)
            for tt in range(NT):
                dve.wait_ge(bqt_mm, tt + 1)
                nc.vector.tensor_copy(QTP[0:64, 0::2, tt * P:(tt + 1) * P],
                                      ps[0:64, 2 * (tt % 2), :].rearrange("p (s n) -> p s n", s=4)).then_inc(bqt_dve, 1)

        def btrans_act(act):
            act.wait_ge(qtp_zero, 1)
            for tt in range(NT):
                act.wait_ge(bqt_mm, tt + 1)
                nc.scalar.copy(QTP[64:128, 1::2, tt * P:(tt + 1) * P],
                               ps[64:128, 2 * (tt % 2), :].rearrange("p (s n) -> p s n", s=4))
                nc.scalar.copy(KTB[:, tt * P:(tt + 1) * P], ps[:, 2 * (tt % 2) + 1, 0:P]).then_inc(bqt_act, 1)

        ITEMS = 8 * NT

        def keys(n):
            return CTX if n // 8 < CT else TOK

        def gqa_pe(pe):
            pe.wait_ge(bqt_dve, NT)
            pe.wait_ge(bqt_act, NT)

            def scores(n):
                if n >= 2:
                    pe.wait_ge(gq_exp, n - 1)
                b, q = 2 * (n % 2), QTP[:, n % 8, n // 8 * P:(n // 8 + 1) * P]
                mm = pe.matmul(ps[:, b, 0:min(512, keys(n))], q, KTB[:, 0:min(512, keys(n))], start=True, stop=True)
                if keys(n) > 512:
                    mm = pe.matmul(ps[:, b + 1, 0:keys(n) - 512], q, KTB[:, 512:keys(n)], start=True, stop=True)
                mm.then_inc(gq_s, 1)

            scores(0)
            for n in range(ITEMS):
                if n + 1 < ITEMS:
                    scores(n + 1)
                pe.wait_ge(gq_exp, n + 1)
                if n >= 1:
                    pe.wait_ge(gq_pta, n)
                    pe.wait_ge(gq_ptd, n)
                nk = keys(n) // P
                for c in range(nk):
                    bank, col = (4 + c // 4, c % 4 * P) if nk > 2 else (4 + c, 0)
                    tr = pe.transpose(ps[:, bank, col:col + P], PB[:, n % 2, c * P:(c + 1) * P], IDENT)
                tr.then_inc(gq_tr, 1)
                if n % 16 == 0 and n >= 16:
                    pe.wait_ge(rows_ok, 3 + n // 16)
                if n == 0:
                    pe.wait_ge(g_act, 1)
                    pe.wait_ge(g_rowT, 1)
                ada_matmuls(pe, 1, U_ADA[1] + n, n, 7)
                pe.wait_ge(gq_pta, n + 1)
                pe.wait_ge(gq_ptd, n + 1)
                if n % 8 == 0 and n >= 8:
                    pe.wait_ge(gq_o, n // 8)
                kv = n % 2
                for c in range(nk):
                    mm = pe.matmul(ps[:, 6, n % 8 * HD:(n % 8 + 1) * HD], PT[:, n % 2, c * P:(c + 1) * P],
                                   VB[:, c, kv * HD:(kv + 1) * HD], start=(c == 0), stop=(c == nk - 1))
                mm.then_inc(gq_pv, 1)

        def gqa_dve(dve, step):
            def copy_p(n):
                dve.wait_ge(gq_tr, n + 1)
                if n >= 2:
                    dve.wait_ge(gq_pv, n - 1)
                m = 512 if keys(n) > CTX else P
                nc.vector.tensor_copy(PT[:, n % 2, 0:m], ps[:, 4, 0:m]).then_inc(gq_ptd, 1)

            def tile_out(tt):
                dve.wait_ge(gq_exp, 8 * tt + 8)
                nc.vector.reciprocal(RINV[:, 8 * tt:8 * tt + 8], RSUM[:, 8 * tt:8 * tt + 8]).then_inc(gq_rinv, 1)
                dve.wait_ge(gq_rinv, tt + 1)
                dve.wait_ge(gq_pv, 8 * tt + 8)
                nc.vector.tensor_tensor(
                    YC[:, tt, 512:1024].rearrange("p (e s d) -> p s e d", e=2, d=HD),
                    ps[:, 6, :].rearrange("p (s e d) -> p s e d", e=2, d=HD),
                    bc(RINV[:, 8 * tt:8 * tt + 8].rearrange("p (s e) -> p s e", e=2).unsqueeze(3), [P, 4, 2, HD]),
                    ALU.mult).then_inc(gq_o, 1)

            for n in range(ITEMS + 1):
                if n < ITEMS:
                    dve.wait_ge(gq_s, n + 1)
                    if n >= 2:
                        dve.wait_ge(gq_exp, n - 1)
                    nc.vector.tensor_reduce(NEGM[:, n % 2:n % 2 + 1],
                                            ps[:, 2 * (n % 2):2 * (n % 2) + 2, :].rearrange("p b n -> p (b n)")[:, 0:keys(n)],
                                            AX, ALU.max, negate=True).then_inc(gq_max, 1)
                if n >= 1:
                    copy_p(n - 1)
                if n >= 1 and n % 8 == 0:
                    tile_out(n // 8 - 1)
                if n >= 1 and n % 16 == 0:
                    ada_rows_dve(dve, 1, n // 16 - 1, 7)

        def gqa_act(act):
            for n in range(ITEMS + 1):
                if n < ITEMS:
                    act.wait_ge(gq_max, n + 1)
                    if n >= 2:
                        act.wait_ge(gq_tr, n - 1)
                    nc.scalar.activation(PB[:, n % 2, 0:keys(n)],
                                         ps[:, 2 * (n % 2):2 * (n % 2) + 2, :].rearrange("p b n -> p (b n)")[:, 0:keys(n)],
                                         ACT.Exp, bias=NEGM[:, n % 2:n % 2 + 1],
                                         accum_out=RSUM[:, n:n + 1]).then_inc(gq_exp, 1)
                if n >= 1:
                    m = n - 1
                    act.wait_ge(gq_tr, m + 1)
                    if m >= 2:
                        act.wait_ge(gq_pv, m - 1)
                    if keys(m) > CTX:
                        nc.scalar.copy(PT[:, m % 2, 512:768], ps[:, 5, 0:256]).then_inc(gq_pta, 1)
                    else:
                        nc.scalar.copy(PT[:, m % 2, P:2 * P], ps[:, 5, 0:P]).then_inc(gq_pta, 1)

        XS = region(16200, 2 * XW, "p (b n) -> p b n", b=2)
        CV = region(16200 + 2 * XW, 2 * XW, "p (b n) -> p b n", b=2)
        CC = region(16200 + 4 * XW, 2 * TOK, "p (b n) -> p b n", b=2)
        QKVT = region(20900, NT * 3 * 512, "p (t n) -> p t n", t=NT)
        cv_zero, cv_x, cv_c, cv_s, cv_tr, cv_outd, cv_outa, cv_xc = (sem(n) for n in (
            "cv_zero", "cv_x", "cv_c", "cv_s", "cv_tr", "cv_outd", "cv_outa", "cv_step"))

        def conv_pe(pe):
            def back(c):
                pe.wait_ge(cv_s, c + 1)
                if c >= 2:
                    pe.wait_ge(cv_outd, c - 1)
                    pe.wait_ge(cv_outa, c - 1)
                b = 4 + 2 * (c % 2)
                for tt in range(NT):
                    bank, col = (b, (tt - CT) * P) if tt >= CT else (b + 1, tt * P)
                    tr = pe.transpose(ps[:, bank, col:col + P], CC[:, c % 2, tt * P:(tt + 1) * P], IDENT)
                tr.then_inc(cv_tr, 1)

            for c in range(CONV_TILES):
                if c >= 2:
                    pe.wait_ge(cv_x, c - 1)
                w = landed(pe, U_CONV + c).rearrange("p (k n) -> p k n", k=KT)
                b = 2 * (c % 2)
                for k in range(KT):
                    pe.matmul(ps[:, b + 1, 0:CTX], w[:, k, :], A[:, k, 0:CTX], start=(k == 0), stop=(k == KT - 1))
                    mm = pe.matmul(ps[:, b, :], w[:, k, :], A[:, k, LO:LO + LAT], start=(k == 0), stop=(k == KT - 1))
                mm.then_inc(w_free, 1)
                if c >= 1:
                    back(c - 1)
            back(CONV_TILES - 1)

        def conv_act(act):
            act.wait_ge(gq_pv, ITEMS)
            act.wait_ge(gq_o, NT)
            act.wait_ge(g_rows, 16)
            act.wait_ge(cv_zero, 1)
            for c in range(CONV_TILES + 2):
                if c < CONV_TILES:
                    act.wait_ge(w_free, U_CONV + c + 1)
                    if c >= 2:
                        act.wait_ge(cv_c, c - 1)
                    nc.scalar.copy(XS[:, c % 2, 1:1 + CTX], ps[:, 2 * (c % 2) + 1, 0:CTX])
                    nc.scalar.copy(XS[:, c % 2, 2 + CTX:2 + TOK], ps[:, 2 * (c % 2), :]).then_inc(cv_x, 1)
                if 1 <= c <= CONV_TILES:
                    m = c - 1
                    act.wait_ge(cv_c, m + 1)
                    if m >= 2:
                        act.wait_ge(cv_tr, m - 1)
                    nc.scalar.activation(CC[:, m % 2, 0:CTX], CV[:, m % 2, 0:CTX], ACT.Silu)
                    nc.scalar.activation(CC[:, m % 2, CTX:TOK], CV[:, m % 2, CTX + 1:TOK + 1], ACT.Silu).then_inc(cv_s, 1)
                if c >= 2:
                    m = c - 2
                    act.wait_ge(cv_tr, m + 1)
                    nc.scalar.copy(QKVT[:, 0:CT, m * P:(m + 1) * P],
                                   ps[:, 5 + 2 * (m % 2), 0:CTX].rearrange("p (t n) -> p t n", n=P)).then_inc(cv_outa, 1)

        def conv_dve(dve):
            step = Chain(dve, cv_xc)
            dve.wait_ge(gq_pv, ITEMS)
            dve.wait_ge(g_rows, 16)
            for g in (0, 1 + CTX, XW - 1):
                last = nc.vector.memset(XS[:, :, g:g + 1], 0.0)
            last.then_inc(cv_zero, 1)
            for c in range(CONV_TILES + 1):
                if c < CONV_TILES:
                    dve.wait_ge(cv_x, c + 1)
                    if c >= 2:
                        dve.wait_ge(cv_s, c - 1)
                    y, x, n = CV[:, c % 2, 0:XW - 2], XS[:, c % 2, :], XW - 2
                    step(nc.vector.tensor_scalar(y, x[:, 0:n], CW[:, c, 0:1], None, ALU.mult))
                    step(nc.vector.scalar_tensor_tensor(y, x[:, 1:n + 1], CW[:, c, 1:2], y, ALU.mult, ALU.add))
                    nc.vector.scalar_tensor_tensor(y, x[:, 2:n + 2], CW[:, c, 2:3], y, ALU.mult, ALU.add).then_inc(cv_c, 1)
                if c >= 1:
                    m = c - 1
                    dve.wait_ge(cv_tr, m + 1)
                    nc.vector.tensor_copy(QKVT[:, CT:NT, m * P:(m + 1) * P],
                                          ps[:, 4 + 2 * (m % 2), :].rearrange("p (t n) -> p t n", n=P)).then_inc(cv_outd, 1)

        MASK = region(0, 2 * MASKS * P, "p (d m n) -> p d m n", d=2, m=MASKS)
        GROW = region(2304, 16 * P, "p (w h n) -> p w h n", w=2, h=8)

        def heads(first, n=P):
            return region(first, 8 * n, "p (h n) -> p h n", h=8)

        E, TT, X, XT, Z, KP = (heads(4352 + 1024 * i) for i in range(6))
        KQ = region(10496, 1024, "p (q w n) -> p q w n", q=4, w=2)
        RV, RW, KTL, QTL, U, VN = (heads(16200 + 512 * i, HD) for i in range(6))
        QTLT, WT = (region(16200 + 512 * i, 512, "p (q n) -> p q n", q=4) for i in (6, 7))
        S = region(30600, 1024, "p (d q n) -> p d q n", d=2, q=4)
        DJ = region(0, 2048, "p (b n) -> p b n", b=2)
        DSS = region(2048, 96 * 3, "p (w n) -> p w n", w=3)
        BEG = region(20300, 96, "p (t d h) -> p t d h", t=NT, d=2)
        ORDER = [(0, 0), (1, 1), (1, 0), (0, 1), (2, 0), (5, 1), (3, 0), (4, 1), (4, 0), (3, 1), (5, 0), (2, 1)]
        LEVELS = 6
        dn_sq, dn_ss, dn_rt, dn_qk, dn_zero, dn_masks, dn_grow = (sem(n) for n in (
            "dn_sq", "dn_ss", "dn_rt", "dn_qk", "dn_zero", "dn_masks", "dn_grow"))
        (dn_t, dn_ka, dn_qd, dn_gram, dn_diff, dn_e, dn_bm, dn_ea, dn_scaled, dn_xt, dn_at, dn_x0t, dn_x0,
         dn_z, dn_zm, dn_xm, dn_xe, dn_qt, dn_qte, dn_uw, dn_wt, dn_ws, dn_vn, dn_o, dn_s) = (
            sem("dn_" + n) for n in ("t ka qd gram diff e bm ea scaled xt at x0t x0 z zm xm xe qt qte uw wt "
                                     "ws vn o s").split())
        dn_xte = sem("dn_xte")
        dn_ok = sem("dn_ok")
        dn_step = sem("dn_step")

        def dnorm_act(act):
            act.wait_ge(cv_tr, CONV_TILES)
            act.wait_ge(cv_outd, CONV_TILES)
            act.wait_ge(cv_outa, CONV_TILES)
            for tt in range(NT):
                if tt >= 2:
                    act.wait_ge(dn_ss, tt - 1)
                nc.scalar.activation(DJ[:, tt % 2, :], QKVT[:, tt, 0:AK], ACT.Square).then_inc(dn_sq, 1)
            act.wait_ge(dn_ss, NT)
            nc.scalar.activation(DSS[:, 1, :], DSS[:, 0, :], ACT.Sqrt, bias=EPSC).then_inc(dn_rt, 1)

        def dnorm_dve(dve):
            step = Chain(dve, dn_step)
            for tt in range(NT):
                dve.wait_ge(dn_sq, tt + 1)
                nc.vector.tensor_reduce(DSS[:, 0, tt * 16:tt * 16 + 16], DJ[:, tt % 2, :].rearrange(
                    "p (h d) -> p h d", d=HD), AX, ALU.add).then_inc(dn_ss, 1)
            dve.wait_ge(dn_rt, 1)
            r = DSS[:, 2, :].rearrange("p (t w h) -> p t w h", t=NT, w=2)
            step(nc.vector.reciprocal(DSS[:, 2, :], DSS[:, 1, :]))
            step(nc.vector.tensor_scalar(r[:, :, 0, :], r[:, :, 0, :], HD ** -0.5, None, ALU.mult))
            step(nc.vector.tensor_tensor(BEG, v4(EG), GB[:, :, :, 1, :], ALU.mult))
            nc.vector.memset(S.rearrange("p d q n -> p (d q n)"), 0.0)
            for tt in range(NT):
                x = QKVT[:, tt, 0:AK].rearrange("p (h d) -> p h d", d=HD)
                nc.vector.tensor_tensor(x, x, bc(DSS[:, 2, tt * 16:tt * 16 + 16].unsqueeze(2), [P, 16, HD]),
                                        ALU.mult).then_inc(dn_qk, 1)

        def dn_pe(pe):
            for i, (tt, d) in enumerate(ORDER):
                if i == 0:
                    pe.wait_ge(dn_qk, NT)
                    pe.wait_ge(cv_x, CONV_TILES)
                else:
                    pe.wait_ge(dn_ok, i)
                for c in range(8):
                    tr = pe.transpose(ps[:, 1 - c // 4, c % 4 * P:(c % 4 + 1) * P], QKVT[:, tt, c * P:(c + 1) * P], IDENT)
                tr.then_inc(dn_t, 1)
                pe.wait_ge(dn_ka, i + 1)
                pe.wait_ge(dn_qd, i + 1)
                for h in range(8):
                    mm = pe.matmul(ps[:, 2 + h // 2, h % 2 * 256:h % 2 * 256 + 256], KP[:, h, :],
                                   KQ[:, h // 2].rearrange("p w n -> p (w n)"), start=True, stop=True)
                mm.then_inc(dn_gram, 1)
                pe.wait_ge(dn_scaled, i + 1)
                for q in range(4):
                    tr = pe.transpose(ps[:, 1, q * P:(q + 1) * P], QTL[:, 2 * q:2 * q + 2, :].rearrange("p h n -> p (h n)"),
                                      IDENT)
                tr.then_inc(dn_qt, 1)
                pe.wait_ge(dn_xt, i + 1)
                for h in range(8):
                    tr = pe.transpose(ps[:, 6 + h // 4, h % 4 * P:(h % 4 + 1) * P], XT[:, h, :], IDENT)
                tr.then_inc(dn_x0t, 1)
                pe.wait_ge(dn_at, i + 1)
                for n in range(LEVELS):
                    v = i * LEVELS + n
                    for g in range(2):
                        if n == 0:
                            pe.wait_ge(dn_x0, i + 1)
                        else:
                            pe.wait_ge(dn_xe, 2 * (i * (LEVELS - 1) + n - 1) + g + 1)
                        for h in range(4 * g, 4 * g + 4):
                            mm = pe.matmul(ps[:, 2 + g, h % 4 * P:(h % 4 + 1) * P], TT[:, h, :], X[:, h, :],
                                           start=True, stop=True)
                        mm.then_inc(dn_z, 1)
                    for g in range(2):
                        pe.wait_ge(dn_zm, 2 * v + g + 1)
                        if v > 0:
                            pe.wait_ge(dn_xte, 2 * (v - 1) + g + 1)
                        for h in range(4 * g, 4 * g + 4):
                            mm = pe.matmul(ps[:, 4 + g, h % 4 * P:(h % 4 + 1) * P], Z[:, h, :], XT[:, h, :],
                                           start=True, stop=True)
                        if n < LEVELS - 1:
                            for h in range(4 * g, 4 * g + 4):
                                mm = pe.matmul(ps[:, 6 + g, h % 4 * P:(h % 4 + 1) * P], XT[:, h, :], Z[:, h, :],
                                               start=True, stop=True)
                        mm.then_inc(dn_xm, 1)
                pe.wait_ge(dn_xte, 2 * LEVELS * (i + 1))
                for h in range(8):
                    pe.matmul(ps[:, 2, h * HD:(h + 1) * HD], XT[:, h, :], RV[:, h, :], start=True, stop=True)
                for h in range(8):
                    mm = pe.matmul(ps[h % 2 * 64:h % 2 * 64 + 64, 3, h // 2 * P:(h // 2 + 1) * P], RW[:, h, :], XT[:, h, :],
                                   start=True, stop=True)
                mm.then_inc(dn_uw, 1)
                pe.wait_ge(dn_wt, i + 1)
                if i >= 2:
                    pe.wait_ge(dn_s, i - 1)
                pe.wait_ge(dn_qte, i + 1)
                for q in range(4):
                    mm = pe.matmul(ps[:, 4, q * P:(q + 1) * P], WT[:, q, :], S[:, d, q, :], start=True, stop=True)
                mm.then_inc(dn_ws, 1)
                for q in range(4):
                    pe.matmul(ps[:, 5, q * P:(q + 1) * P], QTLT[:, q, :], S[:, d, q, :], start=(q == 0), stop=False,
                              skip_group_check=True)
                pe.wait_ge(dn_vn, i + 1)
                for q in range(4):
                    mm = pe.matmul(ps[:, 6, q * P:(q + 1) * P], KTL[:, 2 * q:2 * q + 2, :].rearrange("p h n -> p (h n)"),
                                   VN[:, 2 * q:2 * q + 2, :].rearrange("p h n -> p (h n)"), start=True, stop=True)
                mm.then_inc(dn_o, 1)
                for h in range(8):
                    mm = pe.matmul(ps[:, 5, h * HD:(h + 1) * HD], E[:, h, :], VN[:, h, :], start=False, stop=(h == 7),
                                   skip_group_check=True)
                mm.then_inc(dn_o, 1)

        def pair_halves(ap, par):
            return ap[:, par::2, :]

        def dn_act(act):
            act.wait_ge(dn_zero, 1)
            for i, (tt, d) in enumerate(ORDER):
                act.wait_ge(dn_t, i + 1)
                nc.scalar.copy(KQ[:, :, 0, :], ps[:, 0, :].rearrange("p (q n) -> p q n", q=4))
                for par in range(2):
                    r = slice(64 * par, 64 * par + 64)
                    last = nc.scalar.copy(KP[r, par::2, :], ps[r, 0, :].rearrange("p (q n) -> p q n", q=4))
                last.then_inc(dn_ka, 1)
                act.wait_ge(dn_diff, i + 1)
                nc.scalar.activation(E, E, ACT.Abs).then_inc(dn_e, 1)
                act.wait_ge(dn_e, 2 * i + 1)
                nc.scalar.activation(E, E, ACT.Exp, scale=-1.0).then_inc(dn_e, 1)
                act.wait_ge(dn_qt, i + 1)
                nc.scalar.copy(QTLT.rearrange("p q n -> p (q n)"), ps[:, 1, :]).then_inc(dn_qte, 1)
                act.wait_ge(dn_x0t, i + 1)
                nc.scalar.copy(X.rearrange("p (b h) n -> p b (h n)", b=2), ps[:, 6:8, :]).then_inc(dn_x0, 1)
                for n in range(LEVELS):
                    v = i * LEVELS + n
                    for g in range(2):
                        act.wait_ge(dn_xm, 2 * v + g + 1)
                        nc.scalar.copy(XT[:, 4 * g:4 * g + 4, :].rearrange("p h n -> p (h n)"), ps[:, 4 + g, :]) \
                            .then_inc(dn_xte, 1)
                act.wait_ge(dn_uw, i + 1)
                nc.scalar.copy(WT.rearrange("p q n -> p (q n)"), ps[:, 3, :]).then_inc(dn_wt, 1)

        def dn_dve(dve, step):
            for i, (tt, d) in enumerate(ORDER):
                dve.wait_ge(dn_grow, 16 * (i + 1))
                if i == 0:
                    dve.wait_ge(dn_masks, 16)
                nc.vector.tensor_tensor(E, GROW[:, 0], bc(GB[:, tt, d, 0, :].unsqueeze(2), [P, 8, P]),
                                        ALU.subtract).then_inc(dn_diff, 1)
                dve.wait_ge(dn_t, i + 1)
                nc.vector.tensor_copy(KQ[:, :, 1, :], ps[:, 1, :].rearrange("p (q n) -> p q n", q=4)).then_inc(dn_qd, 1)
                dve.wait_ge(dn_gram, i + 1)
                dve.wait_ge(dn_bm, i + 1)
                gram = ps[:, 2:6, :].rearrange("p b (h w n) -> p (b h) w n", h=2, w=2)
                step(nc.vector.tensor_tensor(TT, gram[:, :, 0, :], TT, ALU.mult))
                step(nc.vector.tensor_tensor(TT, TT, bc(IDENT.unsqueeze(1), [P, 8, P]), ALU.add))
                nc.vector.tensor_tensor(XT, TT, bc(MASK[:, d, 2, :].unsqueeze(1), [P, 8, P]), ALU.mult).then_inc(dn_xt, 1)
                dve.wait_ge(dn_ea, i + 1)
                nc.vector.tensor_tensor(E, gram[:, :, 1, :], E, ALU.mult).then_inc(dn_at, 1)
                for n in range(LEVELS):
                    v = i * LEVELS + n
                    for g in range(2):
                        dve.wait_ge(dn_z, 2 * v + g + 1)
                        nc.vector.tensor_tensor(Z[:, 4 * g:4 * g + 4, :], ps[:, 2 + g, :].rearrange("p (h n) -> p h n", h=4),
                                                bc(MASK[:, d, 3 + n, :].unsqueeze(1), [P, 4, P]), ALU.mult).then_inc(dn_zm, 1)
                    if n < LEVELS - 1:
                        for g in range(2):
                            dve.wait_ge(dn_xm, 2 * v + g + 1)
                            nc.vector.tensor_copy(X[:, 4 * g:4 * g + 4, :].rearrange("p h n -> p (h n)"), ps[:, 6 + g, :]) \
                                .then_inc(dn_xe, 1)
                dve.wait_ge(dn_uw, i + 1)
                step(nc.vector.tensor_copy(U.rearrange("p h n -> p (h n)"), ps[:, 2, :]))
                dve.wait_ge(dn_ws, i + 1)
                nc.vector.tensor_tensor(VN.rearrange("p h n -> p (h n)"), U.rearrange("p h n -> p (h n)"), ps[:, 4, :],
                                        ALU.subtract).then_inc(dn_vn, 1)
                dve.wait_ge(dn_o, 2 * i + 1)
                s8 = S[:, d].rearrange("p q (r n) -> p (q r) n", r=2)
                step(nc.vector.tensor_tensor(s8, s8, bc(v4(EGL)[:, tt, d, :].unsqueeze(2), [P, 8, HD]), ALU.mult))
                for par in range(2):
                    r, cc = slice(64 * par, 64 * par + 64), slice(64 * par, 64 * par + 64)
                    last = nc.vector.tensor_tensor(S[r, d, :, cc], S[r, d, :, cc],
                                                   ps[r, 6, :].rearrange("p (q n) -> p q n", q=4)[:, :, cc], ALU.add)
                last.then_inc(dn_s, 1)
                dve.wait_ge(dn_o, 2 * i + 2)
                o = YC[:, tt, 0:512]
                first = tt not in [a for a, _ in ORDER[:i]]
                if first:
                    nc.vector.tensor_copy(o, ps[:, 5, :]).then_inc(dn_ok, 1)
                else:
                    nc.vector.tensor_tensor(o, ps[:, 5, :], o, ALU.add).then_inc(dn_ok, 1)

        def dn_pool(pool):
            for i, (tt, d) in enumerate(ORDER):
                qkv = QKVT[:, tt, :].rearrange("p (w h n) -> p w h n", w=3, h=8)
                if i == 0:
                    pool.wait_ge(dn_ss, NT)
                    pool.wait_ge(dn_rt, 1)
                    pool.wait_ge(dn_qk, NT)
                    pool.wait_ge(cv_c, CONV_TILES)
                    nc.gpsimd.memset(KP, 0.0).then_inc(dn_zero, 1)
                    pool.dma_start(MASK, t["masks"].rearrange("p (d m n) -> p d m n", d=2, m=MASKS)).then_inc(dn_masks, 16)
                    pool.wait_ge(g_rows, 16)
                else:
                    pool.wait_ge(dn_ok, i)
                pool.dma_start(GROW.rearrange("p w h n -> p (w h) n"),
                               gb_rows[16 * d:16 * d + 16, tt * P:(tt + 1) * P].partition_broadcast(P)).then_inc(dn_grow, 16)

                def col(v):
                    return bc(v.unsqueeze(2), [P, 8, HD])

                nc.gpsimd.tensor_tensor(QTL, qkv[:, 0], col(v4(EG)[:, tt, d, :]), ALU.mult)
                nc.gpsimd.tensor_tensor(KTL, qkv[:, 1], col(v4(EK)[:, tt, d, :]), ALU.mult)
                nc.gpsimd.tensor_tensor(RW, qkv[:, 1], col(BEG[:, tt, d, :]), ALU.mult)
                nc.gpsimd.tensor_tensor(RV, qkv[:, 2], col(GB[:, tt, d, 1, :]), ALU.mult).then_inc(dn_scaled, 1)
                pool.wait_ge(dn_grow, 16 * (i + 1))
                pool.wait_ge(dn_masks, 16)
                nc.gpsimd.tensor_tensor(TT, GROW[:, 1], bc(MASK[:, d, 0, :].unsqueeze(1), [P, 8, P]), ALU.mult) \
                    .then_inc(pool_step, 1)
                pool.wait_ge(pool_step, i + 1)
                pool.wait_ge(dn_e, 2 * i + 2)
                nc.gpsimd.tensor_tensor(TT, TT, E, ALU.mult).then_inc(dn_bm, 1)
                pool.wait_ge(dn_bm, i + 1)
                nc.gpsimd.tensor_tensor(E, E, bc(MASK[:, d, 1, :].unsqueeze(1), [P, 8, P]), ALU.mult).then_inc(dn_ea, 1)

        og_sq, og_ss, og_rt, og_ok, yt_tr, yt_ok, yt_oka, h_back, op_mm, op_ok, op_x = (sem(n) for n in (
            "og_sq", "og_ss", "og_rt", "og_ok", "yt_tr", "yt_ok", "yt_oka", "h_back", "op_mm", "op_ok", "op_x"))
        OJ = region(6400, 1024, "p (b n) -> p b n", b=2)
        OSS = region(7424, 3 * 48, "p (w n) -> p w n", w=3)
        YT = region(0, KT * TOK, "p (k t) -> p k t", k=KT)
        PROD = region(16200, 4 * 512, "p (b n) -> p b n", b=4)

        def gated_act(act):
            for tt in range(NT):
                if tt == 0:
                    act.wait_ge(dn_ok, len(ORDER))
                if tt >= 2:
                    act.wait_ge(og_ss, tt - 1)
                nc.scalar.activation(OJ[:, tt % 2, :], YC[:, tt, 0:512], ACT.Square).then_inc(og_sq, 1)
            act.wait_ge(og_ss, NT)
            nc.scalar.activation(OSS[:, 1, :], OSS[:, 0, :], ACT.Sqrt, bias=EPSC, scale=1.0 / HD).then_inc(og_rt, 1)

        def gated_dve(dve, step):
            for tt in range(NT):
                dve.wait_ge(og_sq, tt + 1)
                nc.vector.tensor_reduce(OSS[:, 0, tt * 8:tt * 8 + 8], OJ[:, tt % 2, :].rearrange("p (h d) -> p h d", d=HD),
                                        AX, ALU.add).then_inc(og_ss, 1)
            dve.wait_ge(og_rt, 1)
            step(nc.vector.reciprocal(OSS[:, 2, :], OSS[:, 1, :]))
            zs = ZS.rearrange("p t (h d) -> p (t h) d", d=HD)
            step(nc.vector.tensor_tensor(zs, zs, bc(GO.unsqueeze(1), [P, NT * 8, HD]), ALU.mult))
            for tt in range(NT):
                o = YC[:, tt, 0:512].rearrange("p (h d) -> p h d", d=HD)
                step(nc.vector.tensor_tensor(o, o, bc(OSS[:, 2, tt * 8:tt * 8 + 8].unsqueeze(2), [P, 8, HD]), ALU.mult))
                nc.vector.tensor_tensor(YC[:, tt, 0:512], YC[:, tt, 0:512], ZS[:, tt, :], ALU.mult).then_inc(og_ok, 1)

        def yt_pe(pe):
            pe.wait_ge(og_ok, NT)
            for k in range(KT):
                if k >= 2:
                    pe.wait_ge(yt_ok, k - 1)
                    pe.wait_ge(yt_oka, k - 1)
                for tt in range(NT):
                    bank, col = (2 * (k % 2) + 1, tt * P) if tt < CT else (2 * (k % 2), (tt - CT) * P)
                    tr = pe.transpose(ps[:, bank, col:col + P], YC[:, tt, k * P:(k + 1) * P], IDENT)
                tr.then_inc(yt_tr, 1)

        def yt_dve(dve):
            for k in range(KT):
                dve.wait_ge(yt_tr, k + 1)
                nc.vector.tensor_copy(YT[:, k, CTX:TOK], ps[:, 2 * (k % 2), :]).then_inc(yt_ok, 1)

        def yt_act(act):
            act.wait_ge(og_ok, NT)
            for k in range(KT):
                act.wait_ge(yt_tr, k + 1)
                nc.scalar.copy(YT[:, k, 0:CTX], ps[:, 2 * (k % 2) + 1, 0:CTX]).then_inc(yt_oka, 1)

        def outproj_pe(pe, u0, tiles, ycols, mm_sem, ok_sem, base=0):
            for j in range(2 * len(tiles)):
                tt, half = tiles[j // 2], j % 2
                if j >= 4:
                    pe.wait_ge(ok_sem, base + j - 3)
                c = ycols(tt)
                for k in range(KT):
                    w = landed(pe, u0 + k)
                    mm = pe.matmul(ps[:, 4 + j % 4, :], c(k), w[:, half * 512:half * 512 + 512],
                                   start=(k == 0), stop=(k == KT - 1))
                    if j == 2 * len(tiles) - 1:
                        mm.then_inc(w_free, 1)
                if j < 2 * len(tiles) - 1:
                    mm.then_inc(mm_sem, 1)

        def outproj_dve(dve, u0, tiles, mm_sem, prod_sem, ok_sem, w, PROD, base=0):
            n = 2 * len(tiles)
            for j in range(n + 1):
                if j < n:
                    tt, half = tiles[j // 2], j % 2
                    if j < n - 1:
                        dve.wait_ge(mm_sem, max(base - 1, 0) + j + 1)
                    else:
                        dve.wait_ge(w_free, u0 + KT)
                    v = 1 if tt < CT else 0
                    nc.vector.tensor_tensor(PROD[:, j % 4, :], ps[:, 4 + j % 4, :], GATE[:, w, v, half * 512:half * 512 + 512],
                                            ALU.mult).then_inc(ok_sem, 1)
                if j >= 1:
                    tt, half = tiles[(j - 1) // 2], (j - 1) % 2
                    dve.wait_ge(ok_sem, base + j)
                    hh = H[:, tt, half * 512:half * 512 + 512]
                    nc.vector.tensor_tensor(hh, hh, PROD[:, (j - 1) % 4, :], ALU.add).then_inc(prod_sem, 1)

        XM = region(0, NT * D, "p (t d) -> p t d", t=NT)
        AM = region(6144, KT * AW, "p (k t) -> p k t", k=KT)
        MJ = region(13312, 2 * D, "p (b d) -> p b d", b=2)
        XP = region(6144, 1024, "p (k s) -> p k s", k=KT)
        XSC = region(7168, 512, "p (k s) -> p k s", k=KT)
        HID, HIDC = region(7680, D), region(8704, D)
        HT = region(9728, 1024, "p (k s) -> p k s", k=KT)
        HTC = region(10752, 512, "p (k s) -> p k s", k=KT)
        STG = region(11264, LAT)
        STGC = region(11776, CTX)
        SH = region(13312, LT * NE * CAP_L, "p (t s) -> p t s", t=LT)
        SHC = region(17408, CT * NE * CAP_C, "p (t s) -> p t s", t=CT)
        ST = region(18432, 8 * LAT, "p (e t) -> p e t", e=8)
        STC = region(22528, 8 * CTX, "p (e t) -> p e t", e=8)
        Y, YX = region(24576, D), region(25600, D)
        SIL, SILC = region(26624, D), region(27648, D)
        WR = region(28672, KT * NE, "p (k e) -> p k e", k=KT)
        LG, AFF, SID = (region(28800 + 96 * i, 96, "p (t e) -> p t e", t=NT) for i in range(3))
        MX = region(29088, 24, "p (w t) -> p w t", w=4)
        TOP = region(29112, 16, "p (b n) -> p b n", b=2)
        WL, WC = region(29128, LAT), region(29640, CTX)
        POS, POSC = region(29896, LAT), region(30408, CTX)
        SG = region(26624, 2048, "p (b s) -> p b s", b=2)

        MOE = "wr lg sm_sub sm_exp aff aft sid sidt sg stt ste".split()
        mo = {n: sem("mo_" + n) for n in MOE}
        pair_sems = ("x_mm xs xsc sil hid ht_mm ht htc yl yc sc_mm sc_ok stg pads").split()
        mp = {n: sem("mp_" + n) for n in pair_sems}
        NPAIR = NE // 2

        def router_pe(pe, l):
            tiles = list(range(NT)) if l == 0 else list(range(CT, NT))
            pe.wait_ge(mo["wr"], 16 * (l + 1))
            n = NORMS[2 * l + 1]
            runs, _, ctx0 = before(n)
            pe.wait_ge(am_ok, KT * (runs + 1))
            if l == 0:
                pe.wait_ge(ac_ok, ctx0 + KT)
            for tt in tiles:
                for k in range(KT):
                    mm = pe.matmul(ps[:, 4, tt * NE:(tt + 1) * NE], AM[:, k, tok_cols(tt):tok_cols(tt) + P], WR[:, k, :],
                                   start=(k == 0), stop=(k == KT - 1))
            mm.then_inc(mo["lg"], 1)
            pe.wait_ge(mo["aff"], l + 1)
            for tt in tiles:
                bank, c = (6, tt * P) if tt < CT else (5, (tt - CT) * P)
                tr = pe.transpose(ps[0:NE, bank, c:c + P], AFF[:, tt, :], IDENT)
            tr.then_inc(mo["aft"], 1)
            pe.wait_ge(mo["sid"], l + 1)
            for tt in tiles:
                src = POSC[0:NE, tt * P:(tt + 1) * P] if tt < CT else POS[0:NE, (tt - CT) * P:(tt - CT + 1) * P]
                tr = pe.transpose(ps[:, 4, tt * NE:(tt + 1) * NE], src, IDENT[0:NE, 0:NE])
            tr.then_inc(mo["sidt"], 1)
            base = l * NT
            for i, tt in enumerate(tiles):
                pe.wait_ge(mo["sg"], base + i + 1)
                if i >= 2:
                    pe.wait_ge(mo["ste"], base + i - 1)
                b = 2 * (i % 2)
                w = 2 * (CAP_C if tt < CT else CAP_L)
                for p in range(NPAIR):
                    tr = pe.transpose(ps[0:w, b + p // 4, p % 4 * P:(p % 4 + 1) * P], SG[:, i % 2, p * w:(p + 1) * w], IDENT)
                tr.then_inc(mo["stt"], 1)

        def router_act(act, l):
            tiles = list(range(NT)) if l == 0 else list(range(CT, NT))
            t0 = tiles[0]
            act.wait_ge(mo["sm_sub"], l + 1)
            nc.scalar.activation(LG[:, t0:, :], LG[:, t0:, :], ACT.Exp).then_inc(mo["sm_exp"], 1)
            base = l * NT
            for i, tt in enumerate(tiles):
                act.wait_ge(mo["stt"], base + i + 1)
                b = 2 * (i % 2)
                if tt < CT:
                    src = ps[0:2 * CAP_C, b:b + 2, :].rearrange("p b (e n) -> p (b e) n", n=P)
                    dst = STC[0:2 * CAP_C, :, tt * P:(tt + 1) * P]
                else:
                    src = ps[:, b:b + 2, :].rearrange("p b (e n) -> p (b e) n", n=P)
                    dst = ST[:, :, (tt - CT) * P:(tt - CT + 1) * P]
                nc.scalar.copy(dst, src).then_inc(mo["ste"], 1)

        def router_dve(dve, l, step):
            tiles = list(range(NT)) if l == 0 else list(range(CT, NT))
            t0, n = tiles[0], len(tiles)
            dve.wait_ge(mo["lg"], l + 1)
            lg = ps[:, 4, t0 * NE:NT * NE].rearrange("p (t e) -> p t e", e=NE)
            step(nc.vector.tensor_reduce(MX[:, 0, t0:NT], lg, AX, ALU.max))
            nc.vector.tensor_tensor(LG[:, t0:, :], lg, bc(MX[:, 0, t0:NT].unsqueeze(2), [P, n, NE]), ALU.subtract) \
                .then_inc(mo["sm_sub"], 1)
            dve.wait_ge(mo["sm_exp"], l + 1)
            step(nc.vector.tensor_reduce(MX[:, 1, t0:NT], LG[:, t0:, :], AX, ALU.add))
            step(nc.vector.reciprocal(MX[:, 2, t0:NT], MX[:, 1, t0:NT]))
            nc.vector.tensor_tensor(AFF[:, t0:, :], LG[:, t0:, :], bc(MX[:, 2, t0:NT].unsqueeze(2), [P, n, NE]), ALU.mult) \
                .then_inc(mo["aff"], 1)
            dve.wait_ge(mo["aft"], l + 1)
            sides = [(WL, POS, 5, LAT, CAP_L)] + ([(WC, POSC, 6, CTX, CAP_C)] if l == 0 else [])
            for b, (work_row, pos, bank, width, cap) in enumerate(sides):
                row = work_row[0:NE, :]
                step(nc.vector.tensor_copy(row, ps[0:NE, bank, 0:width]))
                for r in range(cap // 8):
                    step(nc.vector.max(TOP[0:NE, b, :], row))
                    step(nc.vector.match_replace(row, TOP[0:NE, b, :], row, -1.0))
                step(nc.vector.tensor_scalar(row, row, 0.0, None, ALU.is_lt))
                step(nc.vector.tensor_tensor_scan(pos[0:NE, :], row, row, 0.0, ALU.add, ALU.max))
                last = nc.vector.tensor_tensor(pos[0:NE, :], pos[0:NE, :], row, ALU.mult)
            last.then_inc(mo["sid"], 1)
            dve.wait_ge(mo["sidt"], l + 1)
            step(nc.vector.tensor_copy(SID[:, t0:, :], ps[:, 4, t0 * NE:NT * NE].rearrange("p (t e) -> p t e", e=NE)))
            base = l * NT
            for i, tt in enumerate(tiles):
                cap = CAP_C if tt < CT else CAP_L
                one = SHC[:, tt, :] if tt < CT else SH[:, tt - CT, :]
                one = one.rearrange("p (e s) -> p e s", e=NE)
                step(nc.vector.tensor_tensor(one, bc(SLOT[:, 0:cap].unsqueeze(1), [P, NE, cap]),
                                             bc(SID[:, tt, :].unsqueeze(2), [P, NE, cap]), ALU.is_equal))
                if i >= 2:
                    dve.wait_ge(mo["stt"], base + i - 1)
                nc.vector.tensor_tensor(SG[:, i % 2, 0:NE * cap].rearrange("p (e s) -> p e s", e=NE), one,
                                        bc(AFF[:, tt, :].unsqueeze(2), [P, NE, cap]), ALU.mult).then_inc(mo["sg"], 1)

        SCB = [0, 1, 4, 5]

        def groups(l):
            return [(tt, half) for tt in (range(NT) if l == 0 else range(CT, NT)) for half in range(2)]

        def moe_pe(pe, l, u0):
            ng = len(groups(l))
            P0 = l * NPAIR

            def gather(p):
                for k in range(KT):
                    for tt in range(LT):
                        mm = pe.matmul(ps[:, 2 + k // 4, k % 4 * P:(k % 4 + 1) * P], XM[:, CT + tt, k * P:(k + 1) * P],
                                       SH[:, tt, bass.ds(p * 2 * CAP_L, 2 * CAP_L)], start=(tt == 0), stop=(tt == LT - 1))
                mm.then_inc(mp["x_mm"], 1)
                if l == 0:
                    for k in range(KT):
                        for tt in range(CT):
                            mm = pe.matmul(ps[:, 6, k * 64:(k + 1) * 64], XM[:, tt, k * P:(k + 1) * P],
                                           SHC[:, tt, bass.ds(p * 2 * CAP_C, 2 * CAP_C)], start=(tt == 0), stop=(tt == CT - 1))
                    mm.then_inc(mp["x_mm"], 1)

            nx = 2 if l == 0 else 1
            x0 = 0 if l == 0 else 2 * NPAIR
            ny = 2 if l == 0 else 1

            def product(p, m, lat_src, ctx_src, bank, bank_c, signal):
                for k in range(KT):
                    us = []
                    for e in range(2):
                        j = u0 + 16 * m + 2 * k + e
                        pe.wait_ge(w_land[j % RING], 16 * (j // RING + 1) + p * (16 * 48 // RING))
                        us.append(ring[:, j % RING, :])
                    for n in range(2):
                        for e in range(2):
                            mm = pe.matmul(ps[64 * e:64 * e + 64, bank + n, :], lat_src[:, k, 64 * e:64 * e + 64],
                                           us[e][:, n * 512:(n + 1) * 512], start=(k == 0), stop=(k == KT - 1))
                            if l == 1 and n == 1:
                                mm.then_inc(w_free, 1)
                    if l == 0:
                        for n in range(2):
                            for e in range(2):
                                mm = pe.matmul(ps[32 * e:32 * e + 32, bank_c + n, :], ctx_src[:, k, 32 * e:32 * e + 32],
                                               us[e][:, n * 512:(n + 1) * 512], start=(k == 0), stop=(k == KT - 1))
                                if n == 1:
                                    mm.then_inc(w_free, 1)

            def pair(p, more):
                pe.wait_ge(mp["xs"], P0 + p + 1)
                if l == 0:
                    pe.wait_ge(mp["xsc"], p + 1)
                product(p, 0, XP, XSC, 0, 4, None)
                product(p, 1, XP, XSC, 2, 6, None)
                pe.wait_ge(mp["hid"], ny * p + ny + (l * 2 * NPAIR))
                for k in range(KT):
                    tr = pe.transpose(ps[:, 2 + k // 4, k % 4 * P:(k % 4 + 1) * P], HID[:, k * P:(k + 1) * P], IDENT)
                tr.then_inc(mp["ht_mm"], 1)
                if l == 0:
                    for k in range(KT):
                        tr = pe.transpose(ps[:, 6, k * 64:(k + 1) * 64], HIDC[0:64, k * P:(k + 1) * P], IDENT[0:64, 0:64])
                    tr.then_inc(mp["ht_mm"], 1)
                pe.wait_ge(mp["ht"], P0 + p + 1)
                if l == 0:
                    pe.wait_ge(mp["htc"], p + 1)
                product(p, 2, HT, HTC, 0, 4, None)
                if more:
                    gather(p + 1)
                pe.wait_ge(mp["stg"], P0 + p + 1)
                pe.wait_ge(mp["yl"], P0 + p + 1)
                if l == 0:
                    pe.wait_ge(mp["yc"], p + 1)
                g0 = l * 12 * NPAIR
                for j, (tt, half) in enumerate(groups(l)):
                    if j >= 4:
                        pe.wait_ge(mp["sc_ok"], g0 + ng * p + j - 3)
                    w, y = (STGC[:, tt * P:(tt + 1) * P], YX) if tt < CT else (STG[:, (tt - CT) * P:(tt - CT + 1) * P], Y)
                    pe.matmul(ps[:, SCB[j % 4], :], w, y[:, half * 512:half * 512 + 512], start=True, stop=True) \
                        .then_inc(mp["sc_mm"], 1)
                pe.wait_ge(mp["sc_ok"], g0 + ng * p + ng)

            pe.wait_ge(mo["ste"], NT if l == 0 else NT + LT)
            gather(0)
            with pe.Fori(0, NPAIR - 1) as p:
                pair(p, True)
            pair(NPAIR - 1, False)

        def moe_act(act, l, u0):
            P0 = l * NPAIR
            nx, x0 = (2, 0) if l == 0 else (1, 2 * NPAIR)
            kt0 = 0

            def tokens(p):
                if l == 0:
                    act.wait_ge(mp["x_mm"], 2 * p + 2)
                    for k in range(KT):
                        last = nc.scalar.activation(XSC[:, k, :], ps[:, 6, k * 64:(k + 1) * 64], ACT.Identity,
                                                    scale=AT[:, 1, 1, k:k + 1], bias=modT[:, 1, 3, k:k + 1])
                    last.then_inc(mp["xsc"], 1)

            def pair(p, more):
                act.wait_ge(w_free, u0 + 16 + p * 48)
                nc.scalar.activation(SIL.rearrange("p (b n) -> p b n", b=2), ps[:, 0:2, :], ACT.Silu).then_inc(mp["sil"], 1)
                if l == 0:
                    nc.scalar.activation(SILC[0:64].rearrange("p (b n) -> p b n", b=2), ps[0:64, 4:6, :], ACT.Silu) \
                        .then_inc(mp["sil"], 1)
                act.wait_ge(mp["ht_mm"], x0 + nx * p + 1)
                nc.scalar.copy(HT.rearrange("p (b k) s -> p b (k s)", b=2), ps[:, 2:4, :]).then_inc(mp["ht"], 1)
                if more:
                    tokens(p + 1)

            tokens(0)
            with act.Fori(0, NPAIR - 1) as p:
                pair(p, True)
            pair(NPAIR - 1, False)

        def moe_dve(dve, l, u0):
            P0 = l * NPAIR
            nx, x0 = (2, 0) if l == 0 else (1, 2 * NPAIR)
            g0, ng = l * 12 * NPAIR, len(groups(l))

            def tokens(p):
                dve.wait_ge(mp["x_mm"], x0 + nx * p + 1)
                for k in range(KT):
                    last = nc.vector.tensor_scalar(XP[:, k, :], ps[:, 2 + k // 4, k % 4 * P:(k % 4 + 1) * P],
                                                   AT[:, 1, 0, k:k + 1], modT[:, 0, 3, k:k + 1], ALU.mult, ALU.add)
                last.then_inc(mp["xs"], 1)

            def pair(p, more):
                dve.wait_ge(mp["sil"], x0 + nx * p + nx)
                dve.wait_ge(w_free, u0 + 32 + p * 48)
                nc.vector.tensor_tensor(HID.rearrange("p (b n) -> p b n", b=2), ps[:, 2:4, :],
                                        SIL.rearrange("p (b n) -> p b n", b=2), ALU.mult).then_inc(mp["hid"], 1)
                if l == 0:
                    nc.vector.tensor_tensor(HIDC[0:64].rearrange("p (b n) -> p b n", b=2), ps[0:64, 6:8, :],
                                            SILC[0:64].rearrange("p (b n) -> p b n", b=2), ALU.mult).then_inc(mp["hid"], 1)
                    dve.wait_ge(mp["ht_mm"], 2 * p + 2)
                    nc.vector.tensor_copy(HTC.rearrange("p k s -> p (k s)"), ps[:, 6, :]).then_inc(mp["htc"], 1)
                dve.wait_ge(w_free, u0 + 48 + p * 48)
                nc.vector.tensor_tensor(Y.rearrange("p (b n) -> p b n", b=2), ps[:, 0:2, :],
                                        GATE[:, 1, 0, :].rearrange("p (b n) -> p b n", b=2), ALU.mult).then_inc(mp["yl"], 1)
                if l == 0:
                    nc.vector.tensor_tensor(YX[0:64].rearrange("p (b n) -> p b n", b=2), ps[0:64, 4:6, :],
                                            GATE[0:64, 1, 1, :].rearrange("p (b n) -> p b n", b=2), ALU.mult) \
                        .then_inc(mp["yc"], 1)
                if more:
                    tokens(p + 1)
                for j, (tt, half) in enumerate(groups(l)):
                    dve.wait_ge(mp["sc_mm"], g0 + ng * p + j + 1)
                    hh = H[:, tt, half * 512:half * 512 + 512]
                    nc.vector.tensor_tensor(hh, ps[:, SCB[j % 4], :], hh, ALU.add).then_inc(mp["sc_ok"], 1)

            tokens(0)
            with dve.Fori(0, NPAIR - 1) as p:
                pair(p, True)
            pair(NPAIR - 1, False)

        def moe_pool(pool, l):
            P0 = l * NPAIR
            g0, ng = l * 12 * NPAIR, len(groups(l))
            pool.wait_ge(mo["aft"], l + 1)
            pool.wait_ge(mo["ste"], NT if l == 0 else NT + LT)
            if l == 0:
                nc.gpsimd.memset(STC[64:128].rearrange("p e t -> p (e t)"), 0.0).then_inc(mp["pads"], 1)
                pool.wait_ge(mp["pads"], 1)
                nc.gpsimd.memset(YX[64:128], 0.0).then_inc(mp["pads"], 1)
                pool.wait_ge(mp["pads"], 2)

            def pair(p):
                if l == 0:
                    nc.gpsimd.tensor_copy(STGC, STC[:, bass.ds(p, 1), :].rearrange("p e t -> p (e t)"))
                nc.gpsimd.tensor_copy(STG, ST[:, bass.ds(p, 1), :].rearrange("p e t -> p (e t)")).then_inc(mp["stg"], 1)
                pool.wait_ge(mp["sc_mm"], g0 + ng * p + ng)

            with pool.Fori(0, NPAIR) as p:
                pair(p)

        def moe_sync(sp, l, u0):
            with sp.Fori(0, NPAIR) as p:
                for m, name in enumerate(("expert_w_gate", "expert_w_up", "expert_w_down")):
                    for k in range(KT):
                        for e in range(2):
                            j = u0 + 16 * m + 2 * k + e
                            sp.wait_ge(w_free, j - RING + 1 + p * 48)
                            src = t[name][l].rearrange("(q e) r n -> q e r n", e=2)
                            src = src[bass.ds(p, 1), e, k * P:(k + 1) * P, :].rearrange("q r n -> (q r) n")
                            sp.dma_start(ring[:, j % RING, :], src).then_inc(w_land[j % RING], 16)

        U_MOE = [len(stream), 0]
        all_out, end_ok, fin_in = sem("all_out"), sem("end_ok"), sem("fin_in")
        OP0 = 2 * NT
        OFF = 48 * NPAIR
        U_OQ, U_OK, U_OV, U_OUT1 = (len(stream) + OFF + KT * i for i in range(4))
        for kind in ("oq", "ok", "wv", "wout1"):
            for c in range(KT):
                add(kind, c)
        U_MOE[1] = len(stream) + OFF

        AO = region(0, KT * AW, "p (k t) -> p k t", k=KT)
        QO = region(7168, OH * LAT, "p (h t) -> p h t", h=OH)
        KO = region(15360, KT * AW, "p (c t) -> p c t", c=KT)
        VO = region(22528, 7 * D, "p (m n) -> p m n", m=7)
        XNO = region(22528, NT * D, "p (t d) -> p t d", t=NT)
        OJUNK = region(15360, 2 * D, "p (b d) -> p b d", b=2)
        BIAS = region(0, 4 * 1024, "p (q h n) -> p q h n", q=4, h=4)
        OP = region(4096, 2 * 512, "p (b n) -> p b n", b=2)
        OPT = region(5120, 2 * 512, "p (b n) -> p b n", b=2)
        OPROD = region(0, 4 * 512, "p (b n) -> p b n", b=4)
        OB = region(29696, 2 * 512, "p (b n) -> p b n", b=2)
        YR = region(15360, KT * LAT, "p (k t) -> p k t", k=KT)
        OSUM, OINV, ONEG = region(30720, 64), region(30784, 64), region(30848, 4)
        FING = region(31100, D)
        YO = QO
        o_zero, o_da, o_ac, o_vmm, o_yt, o_yc = (sem(n) for n in ("o_zero", "o_da", "o_ac", "o_vmm", "o_yt", "o_yc"))
        o_bias = [sem(f"o_bias{s}") for s in range(4)]
        GB0 = ITEMS
        GO0 = NT
        OITEMS = LT * OH
        SBANK = [0, 1, 2]

        def v_cols(m):
            return m * P if m < CT else CTX + (m - CT) * P

        def oproj_pe(pe):
            n = before("n1_1")
            pe.wait_ge(am_ok, KT * (n[0] + 1))
            pe.wait_ge(ac_ok, n[2] + KT)
            for c in range(KT):
                w = landed(pe, U_OQ + c).rearrange("p (k n) -> p k n", k=KT)
                if c >= 4:
                    pe.wait_ge(o_ac, c - 3)
                for k in range(KT):
                    mm = pe.matmul(ps[:, c % 4, :], w[:, k, :], AO[:, k, LO:LO + LAT], start=(k == 0), stop=(k == KT - 1))
                mm.then_inc(w_free, 1)
            for c in range(KT):
                w = landed(pe, U_OK + c).rearrange("p (k n) -> p k n", k=KT)
                b = 4 + 2 * (c % 2)
                if c >= 2:
                    pe.wait_ge(o_da, c - 1)
                for k in range(KT):
                    pe.matmul(ps[:, b + 1, 0:CTX], w[:, k, :], AO[:, k, 0:CTX], start=(k == 0), stop=(k == KT - 1))
                    mm = pe.matmul(ps[:, b, :], w[:, k, :], AO[:, k, LO:LO + LAT], start=(k == 0), stop=(k == KT - 1))
                mm.then_inc(w_free, 1)
            for m in range(7):
                for half in range(2):
                    if half == 0:
                        if m >= 2:
                            pe.wait_ge(o_da, KT + m - 1)
                        elif m == 0:
                            pe.wait_ge(o_ac, KT)
                    elif m >= 2:
                        pe.wait_ge(o_ac, KT + m - 1)
                    for k in range(KT):
                        w = landed(pe, U_OV + k)
                        mm = pe.matmul(ps[:, 2 * (m % 2) + half, :], AO[:, k, v_cols(m):v_cols(m) + P],
                                       w[:, half * 512:half * 512 + 512], start=(k == 0), stop=(k == KT - 1))
                        if m == 6 and half == 1:
                            mm.then_inc(w_free, 1)
                    if not (m == 6 and half == 1):
                        mm.then_inc(o_vmm, 1)

        def oproj_act(act):
            act.wait_ge(o_zero, 1)
            for c in range(KT):
                act.wait_ge(w_free, U_OQ + c + 1)
                for par in range(2):
                    r = slice(64 * par, 64 * par + 64)
                    last = nc.scalar.activation(QO[r, 2 * c + par, :], ps[r, c % 4, :], ACT.Copy, scale=HD ** -0.5)
                last.then_inc(o_ac, 1)
            for m in range(7):
                if m < 6:
                    act.wait_ge(o_vmm, 2 * m + 2)
                else:
                    act.wait_ge(w_free, U_OV + KT)
                nc.scalar.copy(VO[:, m, 512:1024], ps[:, 2 * (m % 2) + 1, :]).then_inc(o_ac, 1)

        def oproj_dve(dve):
            nc.vector.memset(KO[:, :, CTX:LO], 0.0)
            nc.vector.memset(KO[:, :, LO + LAT:AW], 0.0)
            for c in range(KT):
                dve.wait_ge(w_free, U_OK + c + 1)
                b = 4 + 2 * (c % 2)
                nc.vector.tensor_copy(KO[:, c, 0:CTX], ps[:, b + 1, 0:CTX])
                nc.vector.tensor_copy(KO[:, c, LO:LO + LAT], ps[:, b, :]).then_inc(o_da, 1)
            for m in range(7):
                dve.wait_ge(o_vmm, 2 * m + 1)
                nc.vector.tensor_copy(VO[:, m, 0:512], ps[:, 2 * (m % 2), :]).then_inc(o_da, 1)

        def oatt_pe(pe):
            pe.wait_ge(o_da, KT + 7)
            pe.wait_ge(o_ac, KT + 7)

            def scores(n):
                if n >= 3:
                    pe.wait_ge(gq_exp, GB0 + n - 2)
                j, h = n // OH, n % OH
                b, q = SBANK[n % 3], QO[:, h, j * P:(j + 1) * P]
                pe.matmul(ps[:, b, 0:CTX], q, KO[:, h // 2, 0:CTX], start=True, stop=True)
                pe.matmul(ps[:, b, CTX:512], q, KO[:, h // 2, CTX + j * P:2 * CTX + j * P], start=True, stop=True) \
                    .then_inc(gq_s, 1)

            def turn(n):
                pe.wait_ge(gq_exp, GB0 + n + 1)
                if n >= 2:
                    pe.wait_ge(gq_pta, GB0 + n - 1)
                for c in range(4):
                    tr = pe.transpose(ps[:, 3 + n % 2, c * P:(c + 1) * P], OP[:, n % 2, c * P:(c + 1) * P], IDENT)
                tr.then_inc(gq_tr, 1)

            def values(n):
                j, h, g = n // OH, n % OH, n // 8
                pe.wait_ge(gq_pta, GB0 + n + 1)
                if n % 8 == 0 and g >= 2:
                    pe.wait_ge(gq_o, GO0 + g - 1)
                for c in range(4):
                    m = c if c < 2 else CT + j + c - 2
                    mm = pe.matmul(ps[:, 5 + g % 2, n % 8 * HD:(n % 8 + 1) * HD], OPT[:, n % 2, c * P:(c + 1) * P],
                                   VO[:, m, h * HD:(h + 1) * HD], start=(c == 0), stop=(c == 3))
                mm.then_inc(gq_pv, 1)

            def turn_heads(g):
                pe.wait_ge(gq_o, GO0 + g + 1)
                if g >= 1:
                    pe.wait_ge(o_yc, g)
                for i in range(4):
                    tr = pe.transpose(ps[:, 7, i * P:(i + 1) * P], OB[:, g % 2, i * P:(i + 1) * P], IDENT)
                tr.then_inc(o_yt, 1)

            scores(0)
            scores(1)
            for n in range(OITEMS + 3):
                if n + 2 < OITEMS:
                    scores(n + 2)
                if n < OITEMS:
                    turn(n)
                if 1 <= n <= OITEMS:
                    values(n - 1)
                if n >= 10 and n % 8 == 2:
                    turn_heads(n // 8 - 1)

        def oatt_dve(dve, step):
            def heads_out(g):
                dve.wait_ge(gq_exp, GB0 + 8 * g + 8)
                nc.vector.reciprocal(OINV[:, 8 * g:8 * g + 8], OSUM[:, 8 * g:8 * g + 8]).then_inc(gq_rinv, 1)
                dve.wait_ge(gq_rinv, GO0 + g + 1)
                dve.wait_ge(gq_pv, GB0 + 8 * g + 8)
                if g >= 2:
                    dve.wait_ge(o_yt, g - 1)
                nc.vector.tensor_tensor(OB[:, g % 2, :].rearrange("p (h d) -> p h d", d=HD),
                                        ps[:, 5 + g % 2, :].rearrange("p (h d) -> p h d", d=HD),
                                        bc(OINV[:, 8 * g:8 * g + 8].unsqueeze(2), [P, 8, HD]), ALU.mult).then_inc(gq_o, 1)

            def turned(g):
                dve.wait_ge(o_yt, g + 1)
                j, half = g // 2, g % 2
                nc.vector.tensor_copy(YO[:, 4 * half:4 * half + 4, j * P:(j + 1) * P],
                                      ps[:, 7, :].rearrange("p (k n) -> p k n", k=4)).then_inc(o_yc, 1)

            for n in range(OITEMS + 4):
                if n < OITEMS:
                    j, h = n // OH, n % OH
                    q = n // 4
                    dve.wait_ge(gq_s, GB0 + n + 1)
                    if n % 4 == 0:
                        dve.wait_ge(o_bias[q % 4], 16 * (q // 4 + 1))
                    loc = ps[:, SBANK[n % 3], CTX:512]
                    step(nc.vector.tensor_tensor(loc, loc, BIAS[:, q % 4, h % 4, :], ALU.add))
                    if n >= 3:
                        dve.wait_ge(gq_exp, GB0 + n - 2)
                    nc.vector.tensor_reduce(ONEG[:, n % 3:n % 3 + 1], ps[:, SBANK[n % 3], :], AX, ALU.max,
                                            negate=True).then_inc(gq_max, 1)
                if n >= 9 and n % 8 == 1:
                    heads_out(n // 8 - 1)
                if n >= 11 and n % 8 == 3:
                    turned(n // 8 - 1)

        def rows_dve(dve):
            dve.wait_ge(o_yc, OITEMS // 8)
            for i in range(LT):
                src = YO[:, 0:KT, :].rearrange("p k (c r) -> p k r c", r=8)[:, :, 2 * i:2 * i + 2, :]
                nc.vector.tensor_copy(YR[:, :, i * P:(i + 1) * P].rearrange("p k (r c) -> p k r c", r=2), src) \
                    .then_inc(o_yc, 1)

        def oatt_act(act):
            act.wait_ge(w_free, U_OV + KT)
            for n in range(OITEMS + 1):
                if n < OITEMS:
                    act.wait_ge(gq_max, GB0 + n + 1)
                    if n >= 2:
                        act.wait_ge(gq_tr, GB0 + n - 1)
                    nc.scalar.activation(OP[:, n % 2, :], ps[:, SBANK[n % 3], :], ACT.Exp, bias=ONEG[:, n % 3:n % 3 + 1],
                                         accum_out=OSUM[:, n:n + 1]).then_inc(gq_exp, 1)
                if n >= 1:
                    m = n - 1
                    act.wait_ge(gq_tr, GB0 + m + 1)
                    if m >= 2:
                        act.wait_ge(gq_pv, GB0 + m - 1)
                    nc.scalar.copy(OPT[:, m % 2, :], ps[:, 3 + m % 2, :]).then_inc(gq_pta, 1)

        def odd_pe(pe):
            pe.wait_ge(ada1_in, 32)
            ada_finish_pe(pe, 1, None)
            norm_pe(pe, "n1_1", range(NT), XNO, True)
            oproj_pe(pe)
            oatt_pe(pe)

            def ycols(tt):
                pe.wait_ge(o_yc, OITEMS // 8 + tt - CT + 1)
                return lambda k: YR[:, k, (tt - CT) * P:(tt - CT + 1) * P]
            outproj_pe(pe, U_OUT1, list(range(CT, NT)), ycols, op_mm, op_ok, OP0)

        def odd_dve(dve, step):
            ada_finish_dve(dve, 1, step)
            nc.vector.memset(AO[:, :, CTX:LO], 0.0)
            nc.vector.memset(AO[:, :, LO + LAT:AW], 0.0)
            dve.wait_ge(gate_mm, 4 * LB(1) + 4)
            norm_dve(dve, "n1_1", range(NT), XNO, 0, AO, by_column=True)
            oproj_dve(dve)
            oatt_dve(dve, step)
            rows_dve(dve)
            outproj_dve(dve, U_OUT1, list(range(CT, NT)), op_mm, op_x, op_ok, 0, OPROD, OP0)
            dve.wait_ge(op_x, OP0 + 2 * LT)

        def odd_act(act):
            ada_finish_act(act, 1)
            norm_act(act, "n1_1", range(NT), OJUNK, True, 0, AO,
                     lambda act, i: act.wait_ge(mp["sc_ok"], 12 * NPAIR))
            oproj_act(act)
            oatt_act(act)

        def odd_pool(pool):
            pool.wait_ge(mp["sc_ok"], 12 * NPAIR)
            pool.dma_start(SEL, t["sel"].rearrange("p (s m) -> p s m", s=8)).then_inc(ada1_in, 16)
            nc.gpsimd.memset(QO, 0.0).then_inc(o_zero, 1)
            pool.wait_ge(w_free, U_OV + KT)
            for q in range(OITEMS // 4):
                if q >= 4:
                    pool.wait_ge(gq_max, GB0 + 4 * (q - 4) + 4)
                j = q // 4
                kind = (0, 1, 1, 2)[j]
                pool.dma_start(BIAS[:, q % 4], t["bias"][kind, :, 4 * (q % 4):4 * (q % 4) + 4, :]).then_inc(o_bias[q % 4], 16)

        FIN = region(0, LT * D, "p (t d) -> p t d", t=LT)

        def final_act(act):
            act.wait_ge(mp["sc_ok"], 12 * NPAIR + 8 * NPAIR)
            for i in range(LT):
                if i >= 2:
                    act.wait_ge(sq_ok, 3 * NT + LT + i - 1)
                nc.scalar.activation(MJ[:, i % 2, :], H[:, CT + i, :], ACT.Square, accum_out=stat_t[:, i:i + 1]) \
                    .then_inc(sq_ok, 1)
            act.wait_ge(sq_ok, 3 * NT + 2 * LT)
            nc.scalar.activation(stat_t[:, 8:8 + LT], stat_t[:, 0:LT], ACT.Sqrt, bias=EPSC, scale=1.0 / D).then_inc(rt_ok, 1)

        def final_dve(dve):
            dve.wait_ge(rt_ok, 5)
            dve.wait_ge(fin_in, 16)
            nc.vector.reciprocal(stat_t[:, 16:16 + LT], stat_t[:, 8:8 + LT]).then_inc(rc_ok, 1)
            dve.wait_ge(rc_ok, 5)
            for i in range(LT):
                nc.vector.scalar_tensor_tensor(FIN[:, i, :], H[:, CT + i, :], stat_t[:, 16 + i:17 + i], FING,
                                               ALU.mult, ALU.mult).then_inc(end_ok, 1)

        block = ctx.enter_context(nc.Block())

        def stream_units(sp, lo, hi, off):
            for u in range(lo, hi):
                kind, args = stream[u]
                u += off
                if u >= RING:
                    sp.wait_ge(w_free, u - RING + 1)
                slot, sig = ring[:, u % RING, :], w_land[u % RING]
                if kind == "ada":
                    l, n = args
                    sp.dma_start(slot, ada_unit(l, n)[0]).then_inc(sig, 16)
                    if (l, n) == (0, 4):
                        sp.dma_start(H[:, 0:CT, :], t["ctx"].rearrange("(t p) d -> p t d", p=P)).then_inc(x_in, 16)
                        sp.dma_start(H[:, CT:NT, :], t["x"].rearrange("(t p) d -> p t d", p=P)).then_inc(x_in, 16)
                    if (l, n) == (0, 4):
                        sp.dma_start(MSUM, t["masks"].rearrange("p (d m n) -> p d m n", d=2, m=MASKS)[:, :, 1, :]) \
                            .then_inc(masks0_in, 16)
                        for dst, name in ((DTB, "dt_bias"), (ALOG, "a_log"), (GO, "go")):
                            sp.dma_start(dst, t[name].partition_broadcast(P)).then_inc(qtp_load, 16)
                        sp.dma_start(GAIN[:, 0:512].rearrange("p (h d) -> p h d", d=HD),
                                     t["gq"].partition_broadcast(P).unsqueeze(1).broadcast_to([P, 8, HD])).then_inc(qtp_load, 16)
                        sp.dma_start(GAIN[:, 512:640].rearrange("p (h d) -> p h d", d=HD),
                                     t["gk"].partition_broadcast(P).unsqueeze(1).broadcast_to([P, 2, HD])).then_inc(qtp_load, 16)
                        sp.dma_start(ROPE, t["rope"].rearrange("p (t w c) -> p t w c", t=LT, w=2)).then_inc(qtp_load, 16)
                        sp.dma_start(CW, t["cw"].rearrange("p (c w) -> p c w", w=3)).then_inc(qtp_load, 16)
                elif kind == "blk":
                    b, k2 = args
                    N = 2 * WIDTH[b]
                    sp.dma_start(slot[:, 0:N], t[("wrest", "wq", "wz")[b]][k2]).then_inc(sig, 16)
                elif kind == "conv":
                    sp.dma_start(slot, t["wconv"][args[0]]).then_inc(sig, 16)
                elif kind in ("wout0", "wout1", "wv"):
                    sp.dma_start(slot, t[kind][args[0] * P:(args[0] + 1) * P, :]).then_inc(sig, 16)
                else:
                    sp.dma_start(slot, t[kind][args[0]]).then_inc(sig, 16)

        @block.sync
        def _(sp):
            sp.dma_start(base_t[:, :], t["base"]).then_inc(consts_in, 16)
            sp.dma_start(cT, t["cT"]).then_inc(small_in, 16)
            sp.dma_start(lnT_t[:, :], t["lnT"]).then_inc(small_in, 16)
            sp.dma_start(SEL, t["sel"].rearrange("p (s m) -> p s m", s=8)).then_inc(consts_in, 16)
            sp.dma_start(rows_t[:, :], t["adab"][0]).then_inc(rows_in, 16)
            stream_units(sp, 0, U_MOE[0], 0)
            moe_sync(sp, 0, U_MOE[0])
            stream_units(sp, U_MOE[0], len(stream), 48 * NPAIR)
            moe_sync(sp, 1, U_MOE[1])
            for i in range(LT):
                sp.wait_ge(end_ok, i + 1)
                sp.dma_start(out[i * P:(i + 1) * P, :], FIN[:, i, :]).then_inc(all_out, 16)
            sp.wait_ge(all_out, 16 * LT)

        @block.tensor
        def _(pe):
            pe.wait_ge(s_silu, 1)
            for n in range(48):
                ada_matmuls(pe, 0, U_ADA[0] + n, n, n // 16)
            pe.wait_ge(consts_in, 32)
            ada_finish_pe(pe, 0, None)
            norm_pe(pe, "n1_0", range(NT), XN, True)
            proj_pe(pe)
            gates_pe(pe)
            btrans_pe(pe)
            gqa_pe(pe)
            pe.wait_ge(gq_exp, ITEMS)
            pe.wait_ge(gq_o, NT)
            pe.wait_ge(rows_ok, 3 + 3)
            conv_pe(pe)
            dn_pe(pe)
            yt_pe(pe)
            pe.wait_ge(yt_ok, KT)
            pe.wait_ge(yt_oka, KT)
            outproj_pe(pe, U_OUT0, list(range(NT)), lambda tt: lambda k: YT[:, k, tt * P:(tt + 1) * P], op_mm, op_ok)
            norm_pe(pe, "n2_0", range(NT), XM, True)
            router_pe(pe, 0)
            moe_pe(pe, 0, U_MOE[0])
            odd_pe(pe)
            norm_pe(pe, "n2_1", range(CT, NT), XM, False)
            router_pe(pe, 1)
            moe_pe(pe, 1, U_MOE[1])

        @block.vector
        def _(dve):
            step = Chain(dve, dve_step)
            nc.vector.memset(EPSC, EPS)
            nc.vector.memset(ONE, 1.0).then_inc(dve_eps, 1)
            nc.vector.memset(A[:, :, CTX:LO], 0.0)
            nc.vector.memset(A[:, :, LO + LAT:AW], 0.0)
            for r in range(3):
                ada_rows_dve(dve, 0, r, r)
            ada_finish_dve(dve, 0, step)
            norm_dve(dve, "n1_0", range(NT), XN, 0, A)
            proj_dve(dve)
            gates_dve(dve, step)
            bnorm_dve(dve, step)
            btrans_dve(dve)
            gqa_dve(dve, step)
            conv_dve(dve)
            dnorm_dve(dve)
            dn_dve(dve, step)
            gated_dve(dve, step)
            yt_dve(dve)
            dve.wait_ge(h_back, 32)
            outproj_dve(dve, U_OUT0, list(range(NT)), op_mm, op_x, op_ok, 0, PROD)
            dve.wait_ge(op_x, 2 * NT)
            norm_dve(dve, "n2_0", range(NT), XM, 1, AM)
            router_dve(dve, 0, step)
            moe_dve(dve, 0, U_MOE[0])
            odd_dve(dve, step)
            norm_dve(dve, "n2_1", range(CT, NT), XM, 1, AM)
            router_dve(dve, 1, step)
            moe_dve(dve, 1, U_MOE[1])
            final_dve(dve)

        @block.scalar
        def _(act):
            act.wait_ge(small_in, 32)
            act.wait_ge(sT_zero, 1)
            nc.scalar.activation(sT[:, :, 0:2], cT.rearrange("p (k v) -> p k v", v=2), ACT.Silu).then_inc(s_silu, 1)
            def ready(act, i):
                if i == 0:
                    act.wait_ge(x_in, 32)
            ada_finish_act(act, 0)
            norm_act(act, "n1_0", range(NT), JUNK, True, 0, A, ready)
            proj_act(act)
            gates_act(act)
            bnorm_act(act)
            btrans_act(act)
            gqa_act(act)
            conv_act(act)
            dnorm_act(act)
            dn_act(act)
            gated_act(act)
            yt_act(act)
            norm_act(act, "n2_0", range(NT), MJ, True, 1, AM,
                     lambda act, i: act.wait_ge(op_x, 2 * i + 2))
            router_act(act, 0)
            moe_act(act, 0, U_MOE[0])
            odd_act(act)
            norm_act(act, "n2_1", range(CT, NT), MJ, False, 1, AM,
                     lambda act, i: act.wait_ge(op_x, OP0 + 2 * i + 2))
            router_act(act, 1)
            moe_act(act, 1, U_MOE[1])
            final_act(act)

        @block.gpsimd
        def _(pool):
            nc.gpsimd.memset(sT_t[:, :], 0.0).then_inc(sT_zero, 1)
            pool.wait_ge(am_ok, KT)
            nc.gpsimd.memset(QTP, 0.0).then_inc(qtp_zero, 1)
            pool.wait_ge(rows_ok, 3)
            pool.wait_ge(modT_mm, 1)
            pool.wait_ge(gate_mm, 4)
            pool.dma_start(rows_t[:, :], t["adab"][1]).then_inc(ada1_in, 16)
            pool.wait_ge(g_rowT, 1)
            pool.dma_start(gb_rows, ROWT[0:32, :]).then_inc(g_rows, 16)
            dn_pool(pool)
            pool.wait_ge(yt_tr, KT)
            pool.dma_start(H[:, 0:CT, :], t["ctx"].rearrange("(t p) d -> p t d", p=P)).then_inc(h_back, 16)
            pool.dma_start(H[:, CT:NT, :], t["x"].rearrange("(t p) d -> p t d", p=P)).then_inc(h_back, 16)
            pool.wait_ge(gate_ok, 4)
            pool.wait_ge(w_free, U_MOE[0])
            pool.dma_start(WR, t["router"][0].rearrange("p (k e) -> p k e", k=KT)).then_inc(mo["wr"], 16)
            moe_pool(pool, 0)
            odd_pool(pool)
            pool.wait_ge(op_mm, OP0)
            pool.dma_start(FING, t["fin_g"].partition_broadcast(P)).then_inc(fin_in, 16)
            pool.dma_start(WR, t["router"][1].rearrange("p (k e) -> p k e", k=KT)).then_inc(mo["wr"], 16)
            moe_pool(pool, 1)


def kernel(**inputs):
    import concourse.bacc as _bacc
    from concourse.bass_utils import run_bass_kernel_spmd as _run

    arrays = lay_out({name: np.asarray(value) for name, value in inputs.items()})
    nc = _bacc.Bacc("TRN2", target_bir_lowering=False, num_devices=1)
    t = {name: nc.dram_tensor(name, list(value.shape), F32, kind="ExternalInput").ap() for name, value in arrays.items()}
    out = nc.dram_tensor("out", [LAT, D], F32, kind="ExternalOutput").ap()
    build(nc, t, out)
    result = _run(nc, [arrays], core_ids=[0])
    return result.results[0]["out"].reshape(1, LAT, D)
```
